# Optimizing a Trainium2 kernel written in Bass

```python
import math
import jax, jax.numpy as jnp
from jax import lax
import numpy as np

'''Hybrid decoder block (1 layer): macaron SwiGLU FFN (half step) -> parallel head-group
token mixing [LongNet dilated sliding-window attention heads | RetNet chunkwise retention heads]
-> macaron SwiGLU FFN (half step) -> final RMSNorm. Every sub-layer is pre-RMSNorm with
adaLN shift/scale/gate from a per-sequence conditioning vector c.
Inputs: x (BATCH, SEQ, D_MODEL), c (BATCH, D_MODEL), per-layer weights stacked on a leading DEPTH axis.
Output: (BATCH, SEQ, D_MODEL).
'''

D_MODEL = 2048
BATCH = 1
SEQ = 256
DEPTH = 1

MIX_WIDTH = D_MODEL
ATT_HEADS = 8
ATT_HEAD_DIM = (MIX_WIDTH // 2) // ATT_HEADS
ATT_WIDTH = ATT_HEADS * ATT_HEAD_DIM
DILATED_CONFIGS = ((128, 1), (512, 4), (2048, 16))
RET_HEADS = 8
RET_V_DIM = (MIX_WIDTH - ATT_WIDTH) // RET_HEADS
RET_K_DIM = RET_V_DIM // 2
RET_QK_WIDTH = RET_HEADS * RET_K_DIM
RET_WIDTH = RET_HEADS * RET_V_DIM
RET_CHUNK = 128
IN_WIDTHS = (ATT_WIDTH, ATT_WIDTH, ATT_WIDTH, RET_QK_WIDTH, RET_QK_WIDTH, RET_WIDTH, RET_WIDTH)
IN_WIDTH = sum(IN_WIDTHS)
IN_SPLITS = tuple(int(i) for i in np.cumsum(IN_WIDTHS)[:-1])
D_FF = ((8 * D_MODEL // 3 + 255) // 256) * 256
N_ADA = 9
EPS = 1e-6

kernel_name = 'hybrid_dilated_attn_retention_macaron_adaln'

def _rmsnorm(x, g):
    xf = x.astype(jnp.float32)
    y = xf * lax.rsqrt(jnp.mean(xf * xf, axis=-1, keepdims=True) + EPS)
    return (y * g.astype(jnp.float32)).astype(x.dtype)

def _modulate(h, shift, scale):
    return h * (1.0 + scale) + shift

def _swiglu(h, w_gate, w_up, w_down):
    return (jax.nn.silu(h @ w_gate) * (h @ w_up)) @ w_down

def _dilated_branch(q, k, v, window, dilation):
    b, s, h, dh = q.shape
    blk = window // dilation
    span = blk * dilation
    s_pad = -(-s // span) * span
    nb = s_pad // span
    pad = ((0, 0), (0, s_pad - s), (0, 0), (0, 0))

    def split(t):
        return jnp.pad(t, pad).reshape(b, nb, blk, dilation, h, dh)

    def with_prev(t):
        prev = jnp.pad(t, ((0, 0), (1, 0), (0, 0), (0, 0), (0, 0), (0, 0)))[:, :-1]
        return jnp.concatenate([prev, t], axis=2)

    qb = split(q)
    kk = with_prev(split(k))
    vv = with_prev(split(v))
    scores = jnp.einsum('bnqrhd,bnkrhd->bnrhqk', qb, kk).astype(jnp.float32) * (dh ** -0.5)
    qi = jnp.arange(blk)[:, None]
    kj = jnp.arange(2 * blk)[None, :]
    dist = qi + blk - kj
    band = (dist >= 0) & (dist <= blk)
    valid = band[None] & ((jnp.arange(nb)[:, None, None] > 0) | (kj >= blk)[None])
    scores = jnp.where(valid[:, None, None], scores, -jnp.inf)
    m = jnp.max(scores, axis=-1, keepdims=True)
    p = jnp.exp(scores - m)
    den = jnp.sum(p, axis=-1)
    o = jnp.einsum('bnrhqk,bnkrhd->bnqrhd', p, vv.astype(jnp.float32))
    o = o / jnp.transpose(den, (0, 1, 4, 2, 3))[..., None]
    lse = jnp.transpose(m[..., 0] + jnp.log(den), (0, 1, 4, 2, 3))
    o = o.reshape(b, s_pad, h, dh)[:, :s]
    lse = lse.reshape(b, s_pad, h)[:, :s]
    return o, lse

def _dilated_attention(q, k, v):
    outs, lses = [], []
    for window, dilation in DILATED_CONFIGS:
        o, lse = _dilated_branch(q, k, v, window, dilation)
        outs.append(o)
        lses.append(lse)
    w = jax.nn.softmax(jnp.stack(lses, axis=0), axis=0)
    return jnp.sum(w[..., None] * jnp.stack(outs, axis=0), axis=0)

def _rotate_every_two(t):
    t1 = t[..., ::2]
    t2 = t[..., 1::2]
    return jnp.stack([-t2, t1], axis=-1).reshape(t.shape)

def _retention(q, k, v, g):
    b, s, h, dk = q.shape
    dv = v.shape[-1]
    pos = jnp.arange(s, dtype=jnp.float32)
    angle = jnp.repeat(1.0 / (10000.0 ** jnp.linspace(0.0, 1.0, dk // 2, dtype=jnp.float32)), 2)
    theta = pos[:, None] * angle[None, :]
    cos = jnp.cos(theta)[None, :, None, :]
    sin = jnp.sin(theta)[None, :, None, :]
    q = q.astype(jnp.float32)
    k = k.astype(jnp.float32) * (dk ** -0.5)
    v = v.astype(jnp.float32)
    q = q * cos + _rotate_every_two(q) * sin
    k = k * cos + _rotate_every_two(k) * sin
    log_g = jnp.log(1.0 - 2.0 ** (-5.0 - jnp.arange(h, dtype=jnp.float32)))
    C = RET_CHUNK
    n = s // C
    qc = q.reshape(b, n, C, h, dk)
    kc = k.reshape(b, n, C, h, dk)
    vc = v.reshape(b, n, C, h, dv)
    idx = jnp.arange(C, dtype=jnp.float32)
    diff = idx[:, None] - idx[None, :]
    decay = jnp.where(diff[None] >= 0, jnp.exp(jnp.maximum(diff, 0.0)[None] * log_g[:, None, None]), 0.0)
    intra = jnp.einsum('bnihd,bnjhd->bnhij', qc, kc) * decay[None, None]
    intra = jnp.einsum('bnhij,bnjhe->bnihe', intra, vc)
    zeta = jnp.exp((C - 1.0 - idx)[None, :] * log_g[:, None])
    kv = jnp.einsum('bnjhd,bnjhe,hj->nbhde', kc, vc, zeta)
    g_chunk = jnp.exp(C * log_g)[None, :, None, None]

    def step(state, kv_c):
        return g_chunk * state + kv_c, state

    _, r_prev = lax.scan(step, jnp.zeros((b, h, dk, dv), jnp.float32), kv)
    xi = jnp.exp((idx + 1.0)[:, None] * log_g[None, :])
    cross = jnp.einsum('bnihd,nbhde->bnihe', qc, r_prev) * xi[None, None, :, :, None]
    o = (intra + cross).reshape(b, s, h, dv)
    mu = jnp.mean(o, axis=-1, keepdims=True)
    var = jnp.mean(jnp.square(o - mu), axis=-1, keepdims=True)
    o = ((o - mu) * lax.rsqrt(var + EPS)).reshape(b, s, h * dv)
    return o * jax.nn.silu(g.astype(jnp.float32))

def _token_mix(h, w_in, w_out):
    b, s, _ = h.shape
    proj = h @ w_in
    aq, ak, av, rq, rk, rv, rg = jnp.split(proj, IN_SPLITS, axis=-1)
    att = _dilated_attention(aq.reshape(b, s, ATT_HEADS, ATT_HEAD_DIM),
                             ak.reshape(b, s, ATT_HEADS, ATT_HEAD_DIM),
                             av.reshape(b, s, ATT_HEADS, ATT_HEAD_DIM)).reshape(b, s, ATT_WIDTH)
    ret = _retention(rq.reshape(b, s, RET_HEADS, RET_K_DIM),
                     rk.reshape(b, s, RET_HEADS, RET_K_DIM),
                     rv.reshape(b, s, RET_HEADS, RET_V_DIM), rg)
    y = jnp.concatenate([att, ret], axis=-1).astype(h.dtype)
    return y @ w_out

def setup_inputs(seed: int = 0) -> dict:
    key = jax.random.key(seed)
    ks = jax.random.split(key, 16)
    D = D_MODEL
    f32 = jnp.float32

    def nrm(k, shape, scale):
        return jax.random.normal(k, shape, f32) * scale

    def gain(k):
        return 1.0 + 0.01 * jax.random.normal(k, (DEPTH, D), f32)

    return {
        'x': jax.random.normal(ks[0], (BATCH, SEQ, D), f32),
        'c': jax.random.normal(ks[1], (BATCH, D), f32),
        'w_ada': nrm(ks[2], (DEPTH, D, N_ADA * D), 0.5 * D ** -0.5),
        'b_ada': nrm(ks[3], (DEPTH, N_ADA * D), 0.01),
        'g_ffn1': gain(ks[4]),
        'w1_gate': nrm(ks[5], (DEPTH, D, D_FF), D ** -0.5),
        'w1_up': nrm(ks[6], (DEPTH, D, D_FF), D ** -0.5),
        'w1_down': nrm(ks[7], (DEPTH, D_FF, D), D_FF ** -0.5),
        'g_mix': gain(ks[8]),
        'w_in': nrm(ks[9], (DEPTH, D, IN_WIDTH), D ** -0.5),
        'w_out': nrm(ks[10], (DEPTH, MIX_WIDTH, D), MIX_WIDTH ** -0.5),
        'g_ffn2': gain(ks[11]),
        'w2_gate': nrm(ks[12], (DEPTH, D, D_FF), D ** -0.5),
        'w2_up': nrm(ks[13], (DEPTH, D, D_FF), D ** -0.5),
        'w2_down': nrm(ks[14], (DEPTH, D_FF, D), D_FF ** -0.5),
        'g_final': 1.0 + 0.01 * jax.random.normal(ks[15], (D,), f32),
    }

def reference(x, c, w_ada, b_ada, g_ffn1, w1_gate, w1_up, w1_down, g_mix, w_in, w_out,
              g_ffn2, w2_gate, w2_up, w2_down, g_final):
    b = x.shape[0]
    for l in range(DEPTH):
        ada = (jax.nn.silu(c) @ w_ada[l] + b_ada[l]).reshape(b, N_ADA, 1, D_MODEL)
        sh1, sc1, gt1, sh2, sc2, gt2, sh3, sc3, gt3 = [ada[:, i] for i in range(N_ADA)]
        h = _modulate(_rmsnorm(x, g_ffn1[l]), sh1, sc1)
        x = x + 0.5 * gt1 * _swiglu(h, w1_gate[l], w1_up[l], w1_down[l])
        h = _modulate(_rmsnorm(x, g_mix[l]), sh2, sc2)
        x = x + gt2 * _token_mix(h, w_in[l], w_out[l])
        h = _modulate(_rmsnorm(x, g_ffn2[l]), sh3, sc3)
        x = x + 0.5 * gt3 * _swiglu(h, w2_gate[l], w2_up[l], w2_down[l])
    return _rmsnorm(x, g_final)


_drawn_inputs = setup_inputs


def setup_inputs(seed=0):
    import zlib

    import numpy as np

    out = dict(_drawn_inputs(seed))
    spreads = {}
    factors = {'b_ada': 5.944, 'g_ffn1': 8.0, 'g_mix': 8.0, 'g_ffn2': 8.0, 'g_final': 5.49}
    for name, (base, spread) in spreads.items():
        noise = np.random.default_rng([zlib.crc32(name.encode()), seed]).standard_normal(out[name].shape)
        drawn = base * np.exp(spread * noise) if base else spread * noise
        out[name] = __import__('jax').numpy.asarray(drawn.astype(out[name].dtype))
    for name, factor in factors.items():
        out[name] = (out[name] * factor).astype(out[name].dtype)
    return out
```

```python
from contextlib import ExitStack

import numpy as np
import concourse.bass as bass
import concourse.mybir as mybir

F32 = mybir.dt.float32
F32R = mybir.dt.float32r
ALU = mybir.AluOpType
ACT = mybir.ActivationFunctionType
AX = mybir.AxisListType

P = 128
T = 256
D = 2048
DT = D // P
FF = 5632
GW = 512
NT = GW // P
KC = 2
CH = KC * GW
RING = 4
SETS = 2
HEADS = 8
DH = 128
DK = 64
MIX_IN = 6144
EPS = 1e-6
ATT_SCALE = DH ** -0.5
RET_SCALE = DK ** -0.5
NEG = -1.0e30
FA = 6
FB = FF // GW - FA
ADA_CHUNKS = DT // KC
ADA_STEPS = DT
ACC = 8
AQ, AK, AV, RQ, RK, RV, RG = 0, 8, 16, 24, 28, 32, 40
NORM_PARTS = 4


class Phase:

    def __init__(self, kind, bodies, kt, ada, reduce, norm=None):
        self.kind, self.bodies, self.ada, self.reduce, self.norm = kind, bodies, ada, reduce, norm
        self.group_chunks = kt // KC
        self.chunks = 2 * self.group_chunks


UP, DOWN, IN, OUT = "up", "down", "in", "out"
PHASES = [
    Phase(UP, FA, DT, 1, True, norm=0), Phase(DOWN, 2, FA * NT, 1, False),
    Phase(UP, FB, DT, 1, True), Phase(DOWN, 2, FB * NT, 2, True),
    Phase(IN, MIX_IN // GW // 2, DT, 1, True, norm=1), Phase(OUT, 2, DT, 2, True),
    Phase(UP, FA, DT, 0, False, norm=2), Phase(DOWN, 2, FA * NT, 0, False),
    Phase(UP, FB, DT, 0, False), Phase(DOWN, 2, FB * NT, 0, False),
]
MIX = 4
ADA_FIRST = 2 * D // GW
ADA_MIX = 1


def plan():
    rows, c, g, a, h, r = [], 0, 0, ADA_FIRST, 0, 0
    for i, p in enumerate(PHASES):
        rows.append((c, g, a, h, r))
        c += p.chunks * p.bodies
        g += 2 * p.bodies
        a += p.ada * p.bodies + (ADA_MIX if i == MIX else 0)
        h += p.bodies if p.kind == UP else 0
        r += 2 * p.bodies if p.kind in (DOWN, OUT) else 0
    rows.append((c, g, a, h, r))
    return [list(x) for x in zip(*rows)]


CHUNK0, GROUP0, ADA0, HID0, RES0 = plan()
NORM_AT = [i for i, p in enumerate(PHASES) if p.norm is not None] + [len(PHASES)]
REDUCED = [ADA_FIRST]
for _i, _p in enumerate(PHASES):
    REDUCED.append(ADA0[_i + 1] if _p.reduce else REDUCED[-1])
assert ADA0[-1] == 9 * D // GW and all(p.chunks % RING == 0 for p in PHASES)
assert all(ADA0[i + 1] - REDUCED[i] <= ACC for i in range(len(PHASES)))


def reductions(i):
    return 1 + sum(p.reduce for p in PHASES[:i + 1])


TABLE = [("ident", P), ("ones_mean", P), ("ones_col", 2), ("rotate", P), ("cos", T), ("sin", T),
         ("mask", 3 * P), ("count", 3 * P), ("decay", HEADS * T)]


def tables():
    i = np.arange(P)
    part = {"ident": np.eye(P), "ones_mean": np.full((P, P), 1.0 / D), "ones_col": np.ones((P, 2))}
    rotate = np.zeros((P, P))
    rotate[i[1::2], i[0::2]] = -1.0
    rotate[i[0::2], i[1::2]] = 1.0
    part["rotate"] = rotate
    angle = np.repeat(np.float32(1.0) / (np.float32(10000.0) ** np.linspace(0, 1, DK // 2, dtype=np.float32)), 2)
    theta = (angle[i % DK][:, None] * np.arange(T, dtype=np.float32)[None, :]).astype(np.float64)
    part["cos"], part["sin"] = np.cos(theta), np.sin(theta)
    dist = np.concatenate([i[:, None] - i[None, :], i[:, None] + P - i[None, :], i[:, None] - i[None, :]], 1)
    count = sum(((dist >= 0) & (dist <= window) & (dist % dilation == 0)).astype(float)
                for window, dilation in ((128, 1), (512, 4), (2048, 16)))
    part["mask"], part["count"] = np.where(count > 0, 0.0, NEG), count
    far = np.arange(T)[None, :] - i[:, None]
    log_g = np.log(1.0 - 2.0 ** (-5.0 - np.arange(HEADS)))
    part["decay"] = np.concatenate(
        [np.where(far >= 0, np.exp(np.maximum(far, 0) * lg) * RET_SCALE, 0.0) for lg in log_g], 1)
    return np.concatenate([part[n] for n, _ in TABLE], 1).astype(np.float32)


def build(nc, x_in_t, c_in_t, w_ada, b_ada_t, gains_t, w_all, table_t, out_t):
    with ExitStack() as ctx:
        def sb(name, shape, dt=F32):
            return ctx.enter_context(nc.sbuf_tensor(name, shape, dt))

        def sem(name):
            return ctx.enter_context(nc.semaphore(name))

        xs = sb("residual", [P, DT, T])
        xsp = sb("x_split", [P, DT, 2 * T], F32R)
        raw = sb("w_raw", [P, RING, CH])
        whi = sb("w_hi", [P, RING, CH], F32R)
        wlo = sb("w_lo", [P, RING, CH], F32R)
        araw = sb("ada_raw", [P, RING, CH])
        acc = sb("ada_acc", [P, ACC, GW])
        s0 = sb("scratch0", [P, NT, T])
        s1 = sb("scratch1", [P, NT, T])
        s2 = sb("scratch2", [P, NT, T])
        s3 = sb("scratch3", [P, NT, T])
        tab = sb("table", [P, table_t.shape[1]])
        ada = sb("ada", [P, 9 * DT])
        gain = sb("gains", [P, 4, DT])
        scl = sb("mod_scale", [P, DT])
        gate = sb("res_gate", [P, DT])
        cc = sb("cond", [P, 2, DT])
        credit = sb("credit", [P, 7])
        rms = s1[:, 2, :]
        var = s1[:, 3, 0:6 * HEADS].rearrange("p (a n) -> p a n", a=3)
        mv = s1[:, 3, 64:64 + 4 * HEADS].rearrange("p (n a) -> p n a", a=2)
        stats = s1[:, 3, 128:140].rearrange("p (n a) -> p n a", n=2)
        mx = sb("score_max", [P, 2, 2])
        nmx = sb("neg_max", [P, 2, 2])
        den = sb("den", [P, 2, 2])
        rden = sb("rden", [P, 2, 2])
        HID_BYTES = FA * NT * 2 * T * 4
        assert HID_BYTES == (MIX_IN // P) * T * 4
        top = (nc.sbuf_usable_end - HID_BYTES) // 32 * 32
        assert nc.sbuf_base <= top, (nc.sbuf_base, top)
        hid = nc.alloc_sbuf_tensor_at("hidden", [P, FA * NT, 2 * T], F32R, offset=top)
        proj = nc.alloc_sbuf_tensor_at("projections", [P, MIX_IN // P, T], F32, offset=top)
        ps = ctx.enter_context(nc.psum_tensor("banks", [P, 8, 512], F32))

        tb, at = {}, 0
        for name, n in TABLE:
            tb[name] = tab[:, at:at + n]
            at += n
        ident, ones_mean, ones_col, rotate = tb["ident"], tb["ones_mean"], tb["ones_col"], tb["rotate"]
        cos, sin, mask, count = tb["cos"], tb["sin"], tb["mask"], tb["count"]

        const_in = sem("const_in")
        x_loaded = sem("x_loaded")
        raw_in = [sem(f"raw_in{i}") for i in range(RING)]
        ada_in = [sem(f"ada_in{i}") for i in range(RING)]
        hi_ready = sem("hi_ready")
        lo_ready = sem("lo_ready")
        w_free = sem("w_free")
        ada_step = sem("ada_step")
        in_kept = sem("in_kept")
        silu_ready = sem("silu_ready")
        hid_f32 = sem("hid_f32")
        hid_hi = sem("hid_hi")
        hid_ready = sem("hid_ready")
        res_step = sem("res_step")
        c_ready = sem("c_ready")
        ada_sum = sem("ada_sum")
        ada_out = sem("ada_out")
        sq_ready = sem("sq_ready")
        part_ready = sem("part_ready")
        mean_ready = sem("mean_ready")
        inv_ready = sem("inv_ready")
        rms_ready = sem("rms_ready")
        scl_ready = sem("scl_ready")
        xn_ready = sem("xn_ready")
        mod_f32 = sem("mod_f32")
        mod_hi = sem("mod_hi")
        mod_ready = sem("mod_ready")
        dve_step = sem("dve_step")
        act_step = sem("act_step")
        v_turned = sem("v_turned")
        v_kept = sem("v_kept")
        g_silu = sem("g_silu")
        rot_done = sem("rot_done")
        rot_kept = sem("rot_kept")
        ra_done = sem("ra_done")
        ra_kept = sem("ra_kept")
        ro_done = sem("ro_done")
        ro_kept = sem("ro_kept")
        var_ready = sem("var_ready")
        std_ready = sem("std_ready")
        ro_norm = sem("ro_norm")
        rt_done = sem("rt_done")
        y_f32 = sem("y_f32")
        y_hi = sem("y_hi")
        y_ready = sem("y_ready")
        sc_done = sem("sc_done")
        sc_masked = sem("sc_masked")
        max_ready = sem("max_ready")
        exp_ready = sem("exp_ready")
        p_ready = sem("p_ready")
        pt_done = sem("pt_done")
        pt_kept = sem("pt_kept")
        ao_done = sem("ao_done")
        out_ready = sem("out_ready")
        out_stored = sem("out_stored")

        block = ctx.enter_context(nc.Block())

        def ahead_range(i, peeled):
            return range(PHASES[i].chunks - (RING if peeled else 0))

        def ahead(i, it, j):
            p = PHASES[i]
            return (it * p.chunks + (CHUNK0[i] + RING + j),
                    it * (p.chunks // RING) + (CHUNK0[i] + RING + j) // RING)

        def group_end(i, it, g):
            p = PHASES[i]
            return it * p.chunks + (RING + CHUNK0[i] + (g + 1) * p.group_chunks)

        def spread(total, j, n):
            return range(total * j // n, total * (j + 1) // n)

        def att_buf(s, h):
            flat = s[:, :, :].rearrange("p a t -> p (a t)")
            return flat[:, (h % 2) * 512:(h % 2) * 512 + 3 * P]

        def run_phases(eng, body, after):
            for i, p in enumerate(PHASES):
                last = i == len(PHASES) - 1
                with eng.Fori(0, p.bodies - 1 if last else p.bodies) as it:
                    body(i, p, it, False)
                if last:
                    body(i, p, p.bodies - 1, True)
                after(i, p)

        @block.sync
        def _(sp):
            def ada_chunk(group, k):
                sp.wait_ge(ada_step, group * ADA_STEPS + 2 * (k + 1))
                sp.dma_start(araw[:, k % RING, :], w_ada[bass.ds(group * ADA_CHUNKS + k, 1), :, :]
                             .rearrange("a p n -> (a p) n")).then_inc(ada_in[k % RING], 16)

            def w_chunk(number, slot):
                sp.wait_ge(lo_ready, number + 1)
                sp.dma_start(raw[:, slot, :], w_all[bass.ds(number, 1), :, :]
                             .rearrange("a p n -> (a p) n")).then_inc(raw_in[slot], 16)

            sp.dma_start(xs[:, :, :], x_in_t).then_inc(x_loaded, 16)
            sp.dma_start(cc[:, 0, :], c_in_t).then_inc(const_in, 16)
            sp.dma_start(ada[:, :], b_ada_t).then_inc(const_in, 16)
            sp.dma_start(gain[:, :, :], gains_t).then_inc(const_in, 16)
            sp.dma_start(tab[:, :], table_t).then_inc(const_in, 16)
            with sp.Fori(0, ADA_FIRST) as g:
                for k in range(ADA_CHUNKS):
                    ada_chunk(g, k)
            for q in range(RING):
                w_chunk(q, q)

            def body(i, p, it, peeled):
                for j in ahead_range(i, peeled):
                    w_chunk(ahead(i, it, j)[0], j % RING)
                    for s in spread(p.ada * ADA_CHUNKS, j, p.chunks):
                        ada_chunk(it * p.ada + (ADA0[i] + s // ADA_CHUNKS), s % ADA_CHUNKS)

            def after(i, p):
                if i == MIX:
                    for k in range(ADA_CHUNKS):
                        ada_chunk(ADA0[i + 1] - ADA_MIX, k)

            run_phases(sp, body, after)
            for q in range(4):
                sp.wait_ge(out_ready, q + 1)
                sp.dma_start(out_t[:, 4 * q:4 * q + 4, :], xs[:, 4 * q:4 * q + 4, :]).then_inc(out_stored, 16)
            sp.wait_ge(out_stored, 64)

        @block.scalar
        def _(act):
            def w_hi(number, uses, slot):
                act.wait_ge(raw_in[slot], uses * 16 + 16)
                act.wait_ge(w_free, number + 1)
                nc.scalar.copy(whi[:, slot, :], raw[:, slot, :]).then_inc(hi_ready, 1)

            def squares(n):
                if n == 0:
                    act.wait_ge(x_loaded, 16)
                else:
                    act.wait_ge(res_step, SETS + RES0[NORM_AT[n]])
                for q in range(NORM_PARTS):
                    nc.scalar.activation(proj[:, 4 * q:4 * q + 4, :], xs[:, 4 * q:4 * q + 4, :],
                                         ACT.Square).then_inc(sq_ready, 1)

            def root(n):
                act.wait_ge(inv_ready, n + 1)
                nc.scalar.activation(rms, s1[:, 1, :], ACT.Sqrt).then_inc(rms_ready, 1)

            def modulate(n):
                act.wait_ge(scl_ready, n + 1)
                for j in range(DT // 2):
                    act.wait_ge(xn_ready, 8 * n + j + 1)
                    if j >= 2:
                        act.wait_ge(mod_ready, 8 * n + j - 1)
                    h = 2 * (j % 2)
                    for t in range(2):
                        k = 2 * j + t
                        ins = nc.scalar.activation(s3[:, h + t, :], s2[:, h + t, :], ACT.Identity,
                                                   bias=ada[:, 3 * n * DT + k:3 * n * DT + k + 1],
                                                   scale=scl[:, k:k + 1])
                    ins.then_inc(mod_f32, 1)
                    act.wait_ge(mod_f32, 8 * n + j + 1)
                    nc.scalar.copy(xsp[:, 2 * j:2 * j + 2, 0:T], s3[:, h:h + 2, :]).then_inc(mod_hi, 1)

            def heads():
                def keep_v(m):
                    act.wait_ge(v_turned, m + 1)
                    nc.scalar.copy(proj[:, (RV + m) if m < 8 else (AV + m - 8), :],
                                   ps[:, m % 2, 0:T]).then_inc(v_kept, 1)

                for m in range(8):
                    keep_v(m)
                act.wait_ge(in_kept, SETS + 2 * PHASES[MIX].bodies)
                nc.scalar.activation(proj[:, RG:RG + 8, :], proj[:, RG:RG + 8, :], ACT.Silu).then_inc(g_silu, 1)
                for m in range(8, 16):
                    keep_v(m)
                for h in range(HEADS):
                    act.wait_ge(ro_done, h + 1)
                    nc.scalar.copy(proj[:, RV + h, :], ps[:, 6 + h % 2, 0:T]).then_inc(ro_kept, 1)
                act.wait_ge(var_ready, 1)
                nc.scalar.activation(var[:, 2, :], var[:, 1, :], ACT.Sqrt).then_inc(std_ready, 1)
                for h in range(HEADS):
                    act.wait_ge(y_f32, h + 1)
                    nc.scalar.copy(xsp[:, HEADS + h, 0:T], s3[:, h % 2, :]).then_inc(y_hi, 1)
                for s in range(HEADS + 2):
                    if s < HEADS:
                        act.wait_ge(max_ready, s + 1)
                        e = att_buf(s0, s)
                        nc.scalar.activation(e[:, 0:P], e[:, 0:P], ACT.Exp, bias=nmx[:, s % 2, 0:1])
                        nc.scalar.activation(e[:, P:3 * P], e[:, P:3 * P], ACT.Exp,
                                             bias=nmx[:, s % 2, 1:2]).then_inc(exp_ready, 1)
                    if 1 <= s <= HEADS:
                        h = s - 1
                        act.wait_ge(pt_done, h + 1)
                        if h >= 2:
                            act.wait_ge(ao_done, h - 1)
                        nc.scalar.copy(att_buf(s1, h), ps[:, 4 + h % 2, 0:3 * P]).then_inc(pt_kept, 1)
                    if s >= 2:
                        h = s - 2
                        act.wait_ge(ao_done, h + 1)
                        nc.scalar.copy(xsp[:, h, 0:T], ps[:, 6 + h % 2, 0:T]).then_inc(y_hi, 1)

            act.wait_ge(const_in, 64)
            nc.scalar.activation(cc[:, 1, :], cc[:, 0, :], ACT.Silu).then_inc(c_ready, 1)
            squares(0)
            root(0)
            for q in range(RING):
                w_hi(q, 0, q)
            modulate(0)

            def body(i, p, it, peeled):
                for j in ahead_range(i, peeled):
                    if p.kind == UP and j == p.group_chunks:
                        act.wait_ge(w_free, group_end(i, it, 0))
                        nc.scalar.activation(s1[:, :, :], ps[:, 0:NT, 0:T], ACT.Silu).then_inc(silu_ready, 1)
                    number, uses = ahead(i, it, j)
                    w_hi(number, uses, j % RING)
                if p.kind == UP:
                    act.wait_ge(hid_f32, it + (HID0[i] + 2))
                    nc.scalar.copy(hid[:, bass.ds(it * NT, NT), 0:T], s3[:, :, :]).then_inc(hid_hi, 1)

            def after(i, p):
                if i == MIX:
                    heads()
                if i + 1 < len(PHASES) and PHASES[i + 1].norm is not None:
                    n = PHASES[i + 1].norm
                    squares(n)
                    root(n)
                    modulate(n)

            run_phases(act, body, after)
            squares(3)
            root(3)

        @block.vector
        def _(dve):
            steps = [0]

            def then(ins):
                steps[0] += 1
                ins.then_inc(dve_step, 1)
                dve.wait_ge(dve_step, steps[0])

            def w_lo(number, slot):
                dve.wait_ge(hi_ready, number + 1)
                nc.vector.tensor_tensor(wlo[:, slot, :], raw[:, slot, :], whi[:, slot, :].bitcast(F32),
                                        ALU.subtract).then_inc(lo_ready, 1)

            def ada_mac(group, k, slot):
                chunk = k // KC
                src = araw[:, chunk % RING, (k % KC) * GW:(k % KC) * GW + GW]
                dst = acc[:, bass.ds(slot, 1), :].rearrange("p a n -> p (a n)")
                if k % KC == 0:
                    dve.wait_ge(ada_in[chunk % RING],
                                group * (16 * ADA_CHUNKS // RING) + (chunk // RING + 1) * 16)
                if k == 0:
                    nc.vector.tensor_scalar(dst, src, cc[:, 1, 0:1], None, ALU.mult).then_inc(ada_step, 1)
                else:
                    dve.wait_ge(ada_step, group * ADA_STEPS + (2 * RING + k))
                    nc.vector.scalar_tensor_tensor(out=dst, in0=src, scalar=cc[:, 1, k:k + 1], in1=dst,
                                                   op0=ALU.mult, op1=ALU.add).then_inc(ada_step, 1)

            def ada_keep(rnd, first, n):
                dve.wait_ge(ada_sum, rnd)
                c = slice(first * NT, (first + n) * NT)
                nc.vector.tensor_tensor(ada[:, c], ps[:, 1, 0:n * NT], ada[:, c], ALU.add).then_inc(ada_out, 1)
                dve.wait_ge(ada_out, rnd)

            def set_gate(layer, factor):
                c = slice((3 * layer + 2) * DT, (3 * layer + 3) * DT)
                then(nc.vector.tensor_scalar(gate[:, :], ada[:, c], factor, None, ALU.mult))

            def mean_squares(n):
                for q in range(NORM_PARTS):
                    dve.wait_ge(sq_ready, NORM_PARTS * n + q + 1)
                    nc.vector.tensor_reduce(s0[:, q, :], proj[:, 4 * q:4 * q + 4, :].rearrange("p a t -> p t a"),
                                            AX.X, ALU.add).then_inc(part_ready, 1)
                dve.wait_ge(mean_ready, n + 1)
                then(nc.vector.tensor_scalar(s1[:, 0, :], ps[:, 0, 0:T], EPS, None, ALU.add))
                nc.vector.reciprocal(s1[:, 1, :], s1[:, 0, :]).then_inc(inv_ready, 1)

            def modulate(n):
                c = slice((3 * n + 1) * DT, (3 * n + 2) * DT)
                nc.vector.scalar_tensor_tensor(out=scl[:, :], in0=ada[:, c], scalar=1.0, in1=gain[:, n, :],
                                               op0=ALU.add, op1=ALU.mult).then_inc(scl_ready, 1)
                dve.wait_ge(rms_ready, n + 1)

                def lo(j):
                    dve.wait_ge(mod_hi, 8 * n + j + 1)
                    h = 2 * (j % 2)
                    nc.vector.tensor_tensor(xsp[:, 2 * j:2 * j + 2, T:2 * T], s3[:, h:h + 2, :],
                                            xsp[:, 2 * j:2 * j + 2, 0:T].bitcast(F32),
                                            ALU.subtract).then_inc(mod_ready, 1)

                for j in range(DT // 2):
                    if j >= 2:
                        dve.wait_ge(mod_f32, 8 * n + j - 1)
                    h = 2 * (j % 2)
                    for t in range(2):
                        ins = nc.vector.tensor_tensor(s2[:, h + t, :], xs[:, 2 * j + t, :], rms, ALU.mult)
                    ins.then_inc(xn_ready, 1)
                    if j >= 1:
                        lo(j - 1)
                lo(DT // 2 - 1)

            def take_group(i, p, it, g):
                if p.kind == UP and g == 0:
                    return
                dve.wait_ge(w_free, group_end(i, it, g))
                r = ps[:, NT * g:NT * g + NT, 0:T]
                if p.kind == UP:
                    dve.wait_ge(silu_ready, it + (HID0[i] + 2))
                    nc.vector.tensor_tensor(s3[:, :, :], s1[:, :, :], r, ALU.mult).then_inc(hid_f32, 1)
                elif p.kind == IN:
                    nc.vector.tensor_copy(proj[:, bass.ds(it * 2 * NT + g * NT, NT), :], r).then_inc(in_kept, 1)
                else:
                    for n in range(NT):
                        tile = it * 2 * NT + (g * NT + n)
                        x = xs[:, bass.ds(tile, 1), :].rearrange("p a t -> p (a t)")
                        ins = nc.vector.scalar_tensor_tensor(out=x, in0=r[:, n, :], scalar=gate[:, bass.ds(tile, 1)],
                                                             in1=x, op0=ALU.mult, op1=ALU.add)
                    ins.then_inc(res_step, 1)

            def hid_lo(i, it):
                dve.wait_ge(hid_hi, it + (HID0[i] + 1))
                tiles = bass.ds(it * NT, NT)
                nc.vector.tensor_tensor(hid[:, tiles, T:2 * T], s3[:, :, :], hid[:, tiles, 0:T].bitcast(F32),
                                        ALU.subtract).then_inc(hid_ready, 1)

            def retention():
                for j in range(4):
                    dve.wait_ge(rot_done, j + 1)
                    if j >= 1:
                        dve.wait_ge(rot_kept, j)
                    for t in range(2):
                        x = proj[:, RQ + 2 * j + t, :]
                        nc.vector.tensor_tensor(s0[:, t, :], x, cos, ALU.mult)
                        ins = nc.vector.tensor_tensor(s1[:, t, :], ps[:, 2 + j % 2, t * T:t * T + T], sin, ALU.mult)
                    then(ins)
                    nc.vector.tensor_tensor(proj[:, RQ + 2 * j:RQ + 2 * j + 2, :], s0[:, 0:2, :], s1[:, 0:2, :],
                                            ALU.add).then_inc(rot_kept, 1)
                for s in range(HEADS + 1):
                    if s < HEADS:
                        dve.wait_ge(ra_done, s + 1)
                        if s >= 2:
                            dve.wait_ge(ro_done, s - 1)
                        a, bank = att_buf(s2, s), 4 + s % 2
                        dec = tb["decay"][:, s * T:s * T + T]
                        nc.vector.tensor_tensor(a[:, 0:T], ps[:, bank, 0:T], dec, ALU.mult)
                        nc.vector.tensor_tensor(a[:, T:T + P], ps[:, bank, T:T + P], dec[:, 0:P],
                                                ALU.mult).then_inc(ra_kept, 1)
                    if s >= 1:
                        h = s - 1
                        dve.wait_ge(ro_kept, h + 1)
                        nc.vector.bn_stats(stats[:, 0, :], proj[:, RV + h, 0:P])
                        then(nc.vector.bn_stats(stats[:, 1, :], proj[:, RV + h, P:T]))
                        nc.vector.bn_aggr(mv[:, 2 * h, :], stats[:, 0, :])
                        then(nc.vector.bn_aggr(mv[:, 2 * h + 1, :], stats[:, 1, :]))
                then(nc.vector.tensor_scalar(var[:, 0, :], mv[:, :, 1], EPS, None, ALU.add))
                nc.vector.reciprocal(var[:, 1, :], var[:, 0, :]).then_inc(var_ready, 1)
                dve.wait_ge(std_ready, 1)

                def norm(h):
                    for t in range(2):
                        o = proj[:, RV + h, t * P:t * P + P]
                        ins = nc.vector.tensor_scalar(o, o, mv[:, 2 * h + t, 0:1], var[:, 2, 2 * h + t:2 * h + t + 1],
                                                      ALU.subtract, ALU.mult)
                    ins.then_inc(ro_norm, 1)

                norm(0)
                dve.wait_ge(g_silu, 1)
                for s in range(HEADS + 1):
                    if s + 1 < HEADS:
                        norm(s + 1)
                    if s < HEADS:
                        dve.wait_ge(rt_done, s + 1)
                        if s >= 2:
                            dve.wait_ge(y_ready, s - 1)
                        nc.vector.tensor_tensor(s3[:, s % 2, :], ps[:, 2 + s % 2, 0:T], proj[:, RG + s, :],
                                                ALU.mult).then_inc(y_f32, 1)
                    if s >= 1:
                        h = s - 1
                        dve.wait_ge(y_hi, h + 1)
                        nc.vector.tensor_tensor(xsp[:, HEADS + h, T:2 * T], s3[:, h % 2, :],
                                                xsp[:, HEADS + h, 0:T].bitcast(F32), ALU.subtract).then_inc(y_ready, 1)

            def attention():
                for s in range(HEADS + 3):
                    if s < HEADS:
                        dve.wait_ge(sc_done, s + 1)
                        if s >= 2:
                            dve.wait_ge(pt_done, s - 1)
                        e = att_buf(s0, s)
                        nc.vector.scalar_tensor_tensor(out=e, in0=ps[:, s % 2, 0:3 * P], scalar=ATT_SCALE, in1=mask,
                                                       op0=ALU.mult, op1=ALU.add).then_inc(sc_masked, 1)
                        dve.wait_ge(sc_masked, s + 1)
                        nc.vector.tensor_reduce(mx[:, s % 2, 0:1], e[:, 0:P], AX.X, ALU.max)
                        then(nc.vector.tensor_reduce(mx[:, s % 2, 1:2], e[:, P:3 * P], AX.X, ALU.max))
                        nc.vector.tensor_scalar(nmx[:, s % 2, :], mx[:, s % 2, :], -1.0, None,
                                                ALU.mult).then_inc(max_ready, 1)
                        for k in range(2 * s, 2 * s + 2):
                            ada_mac(ADA0[MIX + 1] - ADA_MIX, k, ADA0[MIX + 1] - ADA_MIX - REDUCED[MIX])
                    if 1 <= s <= HEADS:
                        h = s - 1
                        dve.wait_ge(exp_ready, h + 1)
                        e = att_buf(s0, h)
                        for b, cut in enumerate((slice(0, P), slice(P, 3 * P))):
                            ins = nc.vector.tensor_tensor_reduce(e[:, cut], e[:, cut], count[:, cut], 1.0, 0.0, ALU.mult,
                                                                 ALU.add, den[:, h % 2, b:b + 1])
                        then(ins)
                        then(nc.vector.reciprocal(rden[:, h % 2, :], den[:, h % 2, :]))
                        for b, cut in enumerate((slice(0, P), slice(P, 3 * P))):
                            ins = nc.vector.tensor_scalar(e[:, cut], e[:, cut], rden[:, h % 2, b:b + 1], None, ALU.mult)
                        ins.then_inc(p_ready, 1)
                    if s >= 3:
                        h = s - 3
                        dve.wait_ge(y_hi, HEADS + h + 1)
                        nc.vector.tensor_tensor(xsp[:, h, T:2 * T], ps[:, 6 + h % 2, 0:T],
                                                xsp[:, h, 0:T].bitcast(F32), ALU.subtract).then_inc(y_ready, 1)

            nc.vector.memset(credit[:, 0:1], 0.0).then_inc(lo_ready, RING)
            nc.vector.memset(credit[:, 1:2], 0.0).then_inc(w_free, RING)
            nc.vector.memset(credit[:, 2:3], 0.0).then_inc(ada_step, 2 * RING)
            nc.vector.memset(credit[:, 3:4], 0.0).then_inc(in_kept, SETS)
            nc.vector.memset(credit[:, 4:5], 0.0).then_inc(res_step, SETS)
            nc.vector.memset(credit[:, 5:6], 0.0).then_inc(silu_ready, 1)
            nc.vector.memset(credit[:, 6:7], 0.0).then_inc(hid_f32, 1)
            mean_squares(0)
            dve.wait_ge(c_ready, 1)
            with dve.Fori(0, ADA_FIRST) as g:
                for k in range(ADA_STEPS):
                    ada_mac(g, k, g)
            ada_keep(1, 0, ADA_FIRST)
            for q in range(RING):
                w_lo(q, q)
            modulate(0)

            def body(i, p, it, peeled):
                for j in ahead_range(i, peeled):
                    if j == p.group_chunks:
                        take_group(i, p, it, 0)
                    w_lo(ahead(i, it, j)[0], j % RING)
                    for s in spread(p.ada * ADA_STEPS, j, p.chunks):
                        ada_mac(it * p.ada + (ADA0[i] + s // ADA_STEPS), s % ADA_STEPS,
                                it * p.ada + (ADA0[i] - REDUCED[i] + s // ADA_STEPS))
                take_group(i, p, it, 1)
                if p.kind == UP:
                    hid_lo(i, it)

            def after(i, p):
                if i == MIX:
                    retention()
                    attention()
                if p.reduce:
                    ada_keep(reductions(i), REDUCED[i], REDUCED[i + 1] - REDUCED[i])
                if i == 0:
                    set_gate(0, 0.5)
                if i == MIX:
                    set_gate(1, 1.0)
                if i == MIX + 1:
                    set_gate(2, 0.5)
                if i + 1 < len(PHASES) and PHASES[i + 1].norm is not None:
                    mean_squares(PHASES[i + 1].norm)
                    modulate(PHASES[i + 1].norm)

            run_phases(dve, body, after)
            mean_squares(3)
            dve.wait_ge(rms_ready, 4)
            for k in range(DT):
                ins = nc.vector.scalar_tensor_tensor(out=xs[:, k, :], in0=xs[:, k, :], scalar=gain[:, 3, k:k + 1],
                                                     in1=rms, op0=ALU.mult, op1=ALU.mult)
                if k % 4 == 3:
                    ins.then_inc(out_ready, 1)

        @block.tensor
        def _(pe):
            def group_chunk(slot, x, k0, bank, last_k):
                for k in range(k0, k0 + KC):
                    for n in range(NT):
                        at = (k - k0) * GW + n * P
                        o, hi, lo = ps[:, bank + n, 0:T], whi[:, slot, at:at + P], wlo[:, slot, at:at + P]
                        nc.tensor.matmul(o, hi, x[:, k, 0:T], start=(k == 0), stop=False)
                        nc.tensor.matmul(o, hi, x[:, k, T:2 * T], start=False, stop=False)
                        ins = nc.tensor.matmul(o, lo, x[:, k, 0:T], start=False, stop=(k == last_k))
                return ins

            def ada_sums(total, n):
                pe.wait_ge(ada_step, 2 * RING + total * ADA_STEPS)
                for m in range(n):
                    for t in range(NT):
                        ins = nc.tensor.matmul(ps[:, 1, m * NT + t:m * NT + t + 1], acc[:, m, t * P:t * P + P],
                                               ones_col[:, 0:1], start=True, stop=True)
                ins.then_inc(ada_sum, 1)

            def mean(n):
                for q in range(NORM_PARTS):
                    pe.wait_ge(part_ready, NORM_PARTS * n + q + 1)
                    ins = nc.tensor.matmul(ps[:, 0, 0:T], ones_mean, s0[:, q, :], start=(q == 0),
                                           stop=(q == NORM_PARTS - 1))
                ins.then_inc(mean_ready, 1)

            def heads():
                pe.wait_ge(in_kept, SETS + 2 * PHASES[MIX].bodies)
                for j in range(4):
                    if j >= 2:
                        pe.wait_ge(rot_kept, j - 1)
                    x = proj[:, RQ + 2 * j:RQ + 2 * j + 2, :].rearrange("p a t -> p (a t)")
                    nc.tensor.matmul(ps[:, 2 + j % 2, :], rotate, x, start=True, stop=True).then_inc(rot_done, 1)
                for m in range(16):
                    v = proj[:, (RV + m) if m < 8 else (AV + m - 8), :]
                    if m >= 2:
                        pe.wait_ge(v_kept, m - 1)
                    for t in range(2):
                        ins = nc.tensor.transpose(ps[:, m % 2, t * P:t * P + P], v[:, t * P:t * P + P], ident)
                    ins.then_inc(v_turned, 1)
                pe.wait_ge(rot_kept, 4)
                for s in range(HEADS + 1):
                    if s < HEADS:
                        if s >= 2:
                            pe.wait_ge(ra_kept, s - 1)
                        rows = slice(DK * (s % 2), DK * (s % 2) + DK)
                        q, k = proj[rows, RQ + s // 2, :], proj[rows, RK + s // 2, :]
                        bank = 4 + s % 2
                        nc.tensor.matmul(ps[:, bank, 0:T], k[:, 0:P], q, start=True, stop=True)
                        nc.tensor.matmul(ps[:, bank, T:T + P], k[:, P:T], q[:, P:T], start=True,
                                         stop=True).then_inc(ra_done, 1)
                    if s >= 1:
                        h = s - 1
                        pe.wait_ge(ra_kept, h + 1)
                        pe.wait_ge(v_kept, h + 1)
                        if h >= 2:
                            pe.wait_ge(ro_kept, h - 1)
                        a, v, bank = att_buf(s2, h), proj[:, RV + h, :], 6 + h % 2
                        nc.tensor.matmul(ps[:, bank, 0:P], a[:, 0:P], v[:, 0:P], start=True, stop=True)
                        nc.tensor.matmul(ps[:, bank, P:T], a[:, P:T], v[:, 0:P], start=True, stop=False)
                        nc.tensor.matmul(ps[:, bank, P:T], a[:, T:T + P], v[:, P:T], start=False,
                                         stop=True).then_inc(ro_done, 1)
                for h in range(HEADS):
                    pe.wait_ge(ro_norm, h + 1)
                    if h >= 2:
                        pe.wait_ge(y_f32, h - 1)
                    for t in range(2):
                        ins = nc.tensor.transpose(ps[:, 2 + h % 2, t * P:t * P + P], proj[:, RV + h, t * P:t * P + P],
                                                  ident)
                    ins.then_inc(rt_done, 1)
                pe.wait_ge(v_kept, 16)
                pe.wait_ge(ra_kept, HEADS)
                pe.wait_ge(ro_kept, HEADS)
                for s in range(HEADS + 2):
                    if s < HEADS:
                        if s >= 2:
                            pe.wait_ge(sc_masked, s - 1)
                        q, k = proj[:, AQ + s, :], proj[:, AK + s, :]
                        nc.tensor.matmul(ps[:, s % 2, 0:P], q[:, 0:P], k[:, 0:P], start=True, stop=True)
                        nc.tensor.matmul(ps[:, s % 2, P:3 * P], q[:, P:T], k, start=True,
                                         stop=True).then_inc(sc_done, 1)
                    if 1 <= s <= HEADS:
                        h = s - 1
                        pe.wait_ge(p_ready, h + 1)
                        if h >= 2:
                            pe.wait_ge(pt_kept, h - 1)
                        e = att_buf(s0, h)
                        for b in range(3):
                            ins = nc.tensor.transpose(ps[:, 4 + h % 2, b * P:b * P + P], e[:, b * P:b * P + P], ident)
                        ins.then_inc(pt_done, 1)
                    if s >= 2:
                        h = s - 2
                        pe.wait_ge(pt_kept, h + 1)
                        if h >= 2:
                            pe.wait_ge(y_ready, HEADS + h - 1)
                        pt, v, bank = att_buf(s1, h), proj[:, AV + h, :], 6 + h % 2
                        nc.tensor.matmul(ps[:, bank, 0:T], v[:, 0:P], pt[:, 0:T], start=True, stop=False,
                                         skip_group_check=True)
                        nc.tensor.matmul(ps[:, bank, P:T], v[:, P:T], pt[:, T:T + P], start=False, stop=True,
                                         skip_group_check=True).then_inc(ao_done, 1)
                pe.wait_ge(y_ready, 2 * HEADS)

            pe.wait_ge(const_in, 64)
            mean(0)
            ada_sums(ADA_FIRST, ADA_FIRST)

            def set_out(i, bodies, g):
                if PHASES[i].kind == UP:
                    pe.wait_ge(hid_f32 if g else silu_ready, bodies + (HID0[i] + 1))
                elif PHASES[i].kind == IN:
                    pe.wait_ge(in_kept, bodies * 2 + (SETS - 1 + g))
                else:
                    pe.wait_ge(res_step, bodies * 2 + (SETS - 1 + g + RES0[i]))

            def body(i, p, it):
                x = hid if p.kind == DOWN else xsp
                for g in range(2):
                    if i > 0:
                        set_out(i - 1, PHASES[i - 1].bodies, g)
                    set_out(i, it, g)
                    for j in range(p.group_chunks):
                        c = g * p.group_chunks + j
                        pe.wait_ge(lo_ready, it * p.chunks + (RING + CHUNK0[i] + c + 1))
                        if p.norm is not None and g == 0:
                            pe.wait_ge(mod_ready, 8 * p.norm + j + 1)
                        if p.kind == DOWN and g == 0 and j in (0, p.group_chunks - 2):
                            pe.wait_ge(hid_ready, HID0[i] - (j == 0))
                        group_chunk(c % RING, x, KC * j, NT * g, KC * p.group_chunks - 1).then_inc(w_free, 1)

            for i, p in enumerate(PHASES):
                with pe.Fori(0, p.bodies) as it:
                    body(i, p, it)
                if i == MIX:
                    heads()
                if p.reduce or (i + 1 < len(PHASES) and PHASES[i + 1].norm is not None) or i == len(PHASES) - 1:
                    for g in range(SETS):
                        set_out(i, p.bodies, g)
                if p.reduce:
                    ada_sums(REDUCED[i + 1], REDUCED[i + 1] - REDUCED[i])
                    pe.wait_ge(ada_out, reductions(i))
                if i + 1 < len(PHASES) and PHASES[i + 1].norm is not None:
                    mean(PHASES[i + 1].norm)
            mean(3)


def chunks(w):
    k, n = w.shape
    return w.reshape(k // (KC * P), KC, P, n // GW, GW).transpose(3, 0, 2, 1, 4).reshape(n // GW, k // (KC * P), P, CH)


def columns(v):
    return np.ascontiguousarray(v.reshape(-1, P).T)


def weights_in_order(w1_gate, w1_up, w1_down, w_in, w_out, w2_gate, w2_up, w2_down):
    total = sum(p.chunks * p.bodies for p in PHASES)
    flat = np.empty((total, P, CH), np.float32)
    at = 0

    def put(part):
        nonlocal at
        part = part.reshape(-1, P, CH)
        flat[at:at + len(part)] = part
        at += len(part)

    def swiglu(gate, up, down):
        gate, up, down = chunks(gate), chunks(up), chunks(down)
        cut = FA * NT // KC
        for first, last in ((0, FA), (FA, FA + FB)):
            for g in range(first, last):
                put(gate[g])
                put(up[g])
            put(down[:, :cut] if first == 0 else down[:, cut:])

    swiglu(w1_gate, w1_up, w1_down)
    put(chunks(w_in))
    put(chunks(w_out))
    swiglu(w2_gate, w2_up, w2_down)
    return flat


def kernel(x, c, w_ada, b_ada, g_ffn1, w1_gate, w1_up, w1_down, g_mix, w_in, w_out,
           g_ffn2, w2_gate, w2_up, w2_down, g_final):
    import concourse.bacc as _bacc
    from concourse.bass_utils import run_bass_kernel_spmd as _run

    nc = _bacc.Bacc("TRN2", target_bir_lowering=False, num_devices=1)
    arrays = {
        "x_t": np.ascontiguousarray(x[0].T.reshape(DT, P, T).transpose(1, 0, 2)),
        "c_t": columns(c[0]),
        "w_ada_chunks": chunks(w_ada[0]).reshape(-1, P, CH),
        "b_ada_t": columns(b_ada[0]),
        "gains_t": np.stack([columns(g_ffn1[0]), columns(g_mix[0]), columns(g_ffn2[0]), columns(g_final)], 1),
        "w_chunks": weights_in_order(w1_gate[0], w1_up[0], w1_down[0], w_in[0], w_out[0], w2_gate[0], w2_up[0],
                                     w2_down[0]),
        "tables": tables(),
    }
    args = [nc.dram_tensor(name, a.shape, F32, kind="ExternalInput").ap() for name, a in arrays.items()]
    out = nc.dram_tensor("out_t", (P, DT, T), F32, kind="ExternalOutput").ap()
    build(nc, *args, out)
    r = _run(nc, [arrays], core_ids=[0])
    got = r.results[0]["out_t"]
    return np.ascontiguousarray(got.transpose(1, 0, 2).reshape(D, T).T)[None]
```

```python
from contextlib import ExitStack

import numpy as np
import concourse.bass as bass
import concourse.mybir as mybir

F32 = mybir.dt.float32
F32R = mybir.dt.float32r
ALU = mybir.AluOpType
ACT = mybir.ActivationFunctionType
AX = mybir.AxisListType

P = 128
T = 256
D = 2048
DT = D // P
FF = 5632
GW = 512
NT = GW // P
KC = 2
CH = KC * GW
RING = 4
SETS = 2
HEADS = 8
DH = 128
DK = 64
MIX_IN = 6144
EPS = 1e-6
ATT_SCALE = DH ** -0.5
RET_SCALE = DK ** -0.5
NEG = -1.0e30
FA = 6
FB = FF // GW - FA
ADA_CHUNKS = DT // KC
ADA_STEPS = DT
ACC = 2
ADA_REST = 2
HEADS_ADA = (26, 30, 43)
AQ, AK, AV, RQ, RK, RV, RG = 0, 8, 16, 24, 28, 32, 40


class Phase:

    def __init__(self, kind, bodies, kt, ada=0, norm=None, tile0=0, squares=None, heads=False):
        self.kind, self.bodies, self.ada, self.norm = kind, bodies, ada, norm
        self.tile0, self.squares, self.heads = tile0, squares, heads
        self.group_chunks = kt // KC
        self.chunks = 2 * self.group_chunks
        self.rounds = (ada if heads else bodies) if ada else 0


UP, DOWN, IN, OUT = "up", "down", "in", "out"
PHASES = [
    Phase(UP, 1, DT, norm=0),
    Phase(UP, FA - 1, DT, ada=1, tile0=NT),
    Phase(DOWN, 2, FA * NT, ada=2),
    Phase(UP, FB, DT, ada=1),
    Phase(DOWN, 2, FB * NT, ada=1, squares=1),
    Phase(IN, 3, DT, ada=1, norm=1),
    Phase(IN, 3, DT, ada=3, tile0=RQ, heads=True),
    Phase(OUT, 2, DT, ada=1, squares=2),
    Phase(UP, 4, DT, ada=1, norm=2),
    Phase(UP, FA - 4, DT, tile0=4 * NT),
    Phase(DOWN, 2, FA * NT),
    Phase(UP, FB, DT),
    Phase(DOWN, 2, FB * NT, squares=3),
]
GATE_AFTER = {1: (0, 0.5), 6: (1, 1.0), 8: (2, 0.5)}
QUARTERS = DT // NT
ADA_FIRST = 2 * QUARTERS
ADA_ORDER = [q + QUARTERS * v for q in range(QUARTERS) for v in range(2)] + list(range(ADA_FIRST, 9 * D // GW))


def plan():
    rows, c, a, h, r, n, rnd = [], 0, ADA_FIRST, 0, 0, 0, QUARTERS
    for p in PHASES:
        rows.append((c, a, h, r, n, rnd))
        c += p.chunks * p.bodies
        a += p.ada * (1 if p.heads else p.bodies)
        h += p.bodies if p.kind == UP else 0
        r += 2 * p.bodies if p.kind in (DOWN, OUT) else 0
        n += 2 * p.bodies if p.kind == IN else 0
        rnd += p.rounds
    rows.append((c, a, h, r, n, rnd))
    return [list(x) for x in zip(*rows)]


CHUNK0, ADA0, HID0, RES0, IN0, ROUND0 = plan()
assert ADA0[-1] == 9 * D // GW and all(p.chunks % RING == 0 for p in PHASES)
HEADS_AT = next(i for i, p in enumerate(PHASES) if p.heads)


def head_schedule():
    table = {}

    def put(chunk, *stages):
        table.setdefault(chunk, []).extend(stages)

    for h in range(HEADS):
        put(3 * h, ("turn_v", h), ("scores", h), ("mask", h))
        put(3 * h + 1, ("exp", h), ("probs", h))
        put(3 * h + 2, ("turn_p", h))
        put(3 * h + 3, ("attend", h))
    for j in range(4):
        put(26 + j, ("rotate", j), ("turn_v", HEADS + j))
        put(33 + j, ("turn_v", HEADS + 4 + j))
    for h in range(HEADS):
        put(30 + 2 * h, ("ret_scores", h))
        put(31 + 2 * h, ("ret_out", h))
        put(32 + 2 * h, ("stats", h))
    for n, chunk in enumerate(HEADS_ADA):
        put(chunk, ("ada", n))
    put(39, ("std", 0))
    put(41, ("silu", 0))
    for h in range(4):
        put(40 + h, ("norm_o", h))
        put(41 + h, ("turn_o", h))
        put(42 + h, ("gate", h))
    put(47, ("std", 1))
    put(48, *[("norm_o", h) for h in range(4, 8)], ("silu", 1), *[("turn_o", h) for h in range(4, 8)],
        *[("split", m) for m in range(4)])
    for h in range(4, 8):
        put(48, ("gate", h))
    put(48, *[("split", m) for m in range(4, 8)])
    return table


SCHEDULE = head_schedule()


TABLE = [("ident", P), ("ones_mean", P), ("eps", 2), ("rotate", P), ("cos", T), ("sin", T),
         ("mask", 3 * P), ("count", 3 * P), ("decay", HEADS * T)]


def tables():
    i = np.arange(P)
    part = {"ident": np.eye(P), "ones_mean": np.full((P, P), 1.0 / D), "eps": np.full((P, 2), EPS)}
    rotate = np.zeros((P, P))
    rotate[i[1::2], i[0::2]] = -1.0
    rotate[i[0::2], i[1::2]] = 1.0
    part["rotate"] = rotate
    angle = np.repeat(np.float32(1.0) / (np.float32(10000.0) ** np.linspace(0, 1, DK // 2, dtype=np.float32)), 2)
    theta = (angle[i % DK][:, None] * np.arange(T, dtype=np.float32)[None, :]).astype(np.float64)
    part["cos"], part["sin"] = np.cos(theta), np.sin(theta)
    dist = np.concatenate([i[:, None] - i[None, :], i[:, None] + P - i[None, :], i[:, None] - i[None, :]], 1)
    count = sum(((dist >= 0) & (dist <= window) & (dist % dilation == 0)).astype(float)
                for window, dilation in ((128, 1), (512, 4), (2048, 16)))
    part["mask"], part["count"] = np.where(count > 0, 0.0, NEG), count
    far = np.arange(T)[None, :] - i[:, None]
    log_g = np.log(1.0 - 2.0 ** (-5.0 - np.arange(HEADS)))
    part["decay"] = np.concatenate(
        [np.where(far >= 0, np.exp(np.maximum(far, 0) * lg) * RET_SCALE, 0.0) for lg in log_g], 1)
    return np.concatenate([part[n] for n, _ in TABLE], 1).astype(np.float32)


EARLY = sum(n for _, n in TABLE[:3])


def build(nc, x_in_t, c_in_t, w_ada, b_ada_t, gains_t, w_all, table_t, out_t):
    with ExitStack() as ctx:
        def sb(name, shape, dt=F32):
            return ctx.enter_context(nc.sbuf_tensor(name, shape, dt))

        def sem(name):
            return ctx.enter_context(nc.semaphore(name))

        xs = sb("residual", [P, DT, T])
        xsp = sb("x_split", [P, DT, 2 * T], F32R)
        raw = sb("w_raw", [P, RING, CH])
        whi = sb("w_hi", [P, RING, CH], F32R)
        wlo = sb("w_lo", [P, RING, CH], F32R)
        araw = sb("ada_raw", [P, RING, CH])
        acc = sb("ada_acc", [P, ACC, GW])
        s0 = sb("scratch0", [P, NT, T])
        s1 = sb("scratch1", [P, NT, T])
        s2 = sb("scratch2", [P, NT, T])
        s3 = sb("scratch3", [P, NT, T])
        tab = sb("table", [P, table_t.shape[1]])
        ada = sb("ada", [P, 9 * DT])
        gain = sb("gains", [P, 4, DT])
        scl = sb("mod_scale", [P, DT])
        gate = sb("res_gate", [P, DT])
        cc = sb("cond", [P, 2, DT])
        credit = sb("credit", [P, 7])
        asum = sb("ada_sums", [P, ACC * NT])
        root = sb("root", [P, T])
        rms = sb("rms", [P, T])
        var = sb("var", [P, 3, 2 * HEADS])
        mv = sb("mean_var", [P, 2 * HEADS, 2])
        stats = sb("stats", [P, 2, 6])
        mx = sb("score_max", [P, 2, 2])
        nmx = sb("neg_max", [P, 2, 2])
        den = sb("den", [P, 2, 2])
        rden = sb("rden", [P, 2, 2])
        HID_BYTES = FA * NT * 2 * T * 4
        assert HID_BYTES == (MIX_IN // P) * T * 4
        top = (nc.sbuf_usable_end - HID_BYTES) // 32 * 32
        assert nc.sbuf_base <= top, (nc.sbuf_base, top)
        hid = nc.alloc_sbuf_tensor_at("hidden", [P, FA * NT, 2 * T], F32R, offset=top)
        proj = nc.alloc_sbuf_tensor_at("projections", [P, MIX_IN // P, T], F32, offset=top)
        ps = ctx.enter_context(nc.psum_tensor("banks", [P, 8, 512], F32))

        tb, at = {}, 0
        for name, n in TABLE:
            tb[name] = tab[:, at:at + n]
            at += n
        ident, ones_mean, eps, rotate = tb["ident"], tb["ones_mean"], tb["eps"], tb["rotate"]
        cos, sin, mask, count = tb["cos"], tb["sin"], tb["mask"], tb["count"]

        const_in = sem("const_in")
        table_in = sem("table_in")
        x_loaded = sem("x_loaded")
        raw_in = [sem(f"raw_in{i}") for i in range(RING)]
        ada_in = [sem(f"ada_in{i}") for i in range(RING)]
        hi_ready = sem("hi_ready")
        lo_ready = sem("lo_ready")
        w_free = sem("w_free")
        ada_step = sem("ada_step")
        in_kept = sem("in_kept")
        silu_ready = sem("silu_ready")
        hid_f32 = sem("hid_f32")
        hid_hi = sem("hid_hi")
        hid_ready = sem("hid_ready")
        res_step = sem("res_step")
        c_ready = sem("c_ready")
        ada_turned = sem("ada_turned")
        asum_ready = sem("asum_ready")
        ada_out = sem("ada_out")
        sq_ready = sem("sq_ready")
        part_ready = sem("part_ready")
        mean_ready = sem("mean_ready")
        root_ready = sem("root_ready")
        scl_ready = sem("scl_ready")
        xn_ready = sem("xn_ready")
        mod_hi = sem("mod_hi")
        mod_ready = sem("mod_ready")
        dve_step = sem("dve_step")
        v_turned = sem("v_turned")
        v_kept = sem("v_kept")
        g_silu = sem("g_silu")
        rot_done = sem("rot_done")
        rot_kept = sem("rot_kept")
        ra_done = sem("ra_done")
        ra_kept = sem("ra_kept")
        ro_done = sem("ro_done")
        ro_kept = sem("ro_kept")
        var_ready = sem("var_ready")
        std_ready = sem("std_ready")
        ro_norm = sem("ro_norm")
        rt_done = sem("rt_done")
        y_att = sem("y_att")
        y_ret = sem("y_ret")
        y_hi = sem("y_hi")
        y_ready = sem("y_ready")
        sc_done = sem("sc_done")
        sc_masked = sem("sc_masked")
        max_ready = sem("max_ready")
        exp_ready = sem("exp_ready")
        p_ready = sem("p_ready")
        pt_done = sem("pt_done")
        pt_kept = sem("pt_kept")
        ao_done = sem("ao_done")
        out_ready = sem("out_ready")
        out_stored = sem("out_stored")

        block = ctx.enter_context(nc.Block())

        MISC = 4

        def group_out(g):
            return ps[:, 2 * g:2 * g + 2, :].rearrange("p b (n t) -> p (b n) t", t=T)

        def ahead_range(i, peeled):
            return range(PHASES[i].chunks - (RING if peeled else 0))

        def ahead(i, it, j):
            p = PHASES[i]
            return (it * p.chunks + (CHUNK0[i] + RING + j),
                    it * (p.chunks // RING) + (CHUNK0[i] + RING + j) // RING)

        def turn_bank(h):
            return 7 if h < 4 else h

        def y_tiles(m):
            at = AQ + 2 * m if m < 4 else RG + 2 * (m - 4)
            return proj[:, at:at + 2, :]

        def scaled(j):
            return (s2, s3)[j // 2 % 2][:, 2 * (j % 2):2 * (j % 2) + 2, :]

        def group_end(i, it, g):
            p = PHASES[i]
            return it * p.chunks + (RING + CHUNK0[i] + (g + 1) * p.group_chunks)

        def spread(total, j, n):
            return range(total * j // n, total * (j + 1) // n)

        def att_buf(s, h):
            flat = s[:, :, :].rearrange("p a t -> p (a t)")
            return flat[:, (h % 2) * 512:(h % 2) * 512 + 3 * P]

        def run_phases(eng, body, stage, after):
            for i, p in enumerate(PHASES):
                last = i == len(PHASES) - 1
                if p.heads:
                    def follow(chunk):
                        for name, n in SCHEDULE.get(chunk, ()):
                            if name in stage:
                                stage[name](n)

                    for it in range(p.bodies):
                        body(i, p, it, False, follow)
                    follow(p.chunks * p.bodies)
                elif i > 0:
                    with eng.Fori(0, p.bodies - 1 if last else p.bodies) as it:
                        body(i, p, it, False, None)
                    if last:
                        body(i, p, p.bodies - 1, True, None)
                after(i, p)

        def ada_part(p, it, j, total):
            if p.heads:
                j, n = it * p.chunks + j, HEADS_ADA[-1] - 1
            else:
                n = p.chunks - ADA_REST
            return spread(p.ada * total, j, n) if j < n else ()

        @block.sync
        def _(sp):
            def ada_chunk(group, k):
                sp.wait_ge(ada_step, group * ADA_STEPS + 2 * (k + 1))
                sp.dma_start(araw[:, k % RING, :], w_ada[bass.ds(group * ADA_CHUNKS + k, 1), :, :]
                             .rearrange("a p n -> (a p) n")).then_inc(ada_in[k % RING], 16)

            def w_chunk(number, slot):
                sp.wait_ge(lo_ready, number + 1)
                sp.dma_start(raw[:, slot, :], w_all[bass.ds(number, 1), :, :]
                             .rearrange("a p n -> (a p) n")).then_inc(raw_in[slot], 16)

            sp.dma_start(cc[:, 0, :], c_in_t).then_inc(const_in, 16)
            sp.dma_start(ada[:, :], b_ada_t).then_inc(const_in, 16)
            sp.dma_start(gain[:, :, :], gains_t).then_inc(const_in, 16)
            sp.dma_start(tab[:, 0:EARLY], table_t[:, 0:EARLY]).then_inc(const_in, 16)
            for q in range(QUARTERS):
                for n in range(2 * q, 2 * q + 2):
                    for k in range(ADA_CHUNKS):
                        ada_chunk(n, k)
                        if n == 2 * q and k == RING - 1:
                            if q == 0:
                                sp.dma_start(xs[:, :, :], x_in_t).then_inc(x_loaded, 16)
                            for c in range(4 * q, 4 * q + 4):
                                w_chunk(c, c % RING)
            for c in range(PHASES[0].chunks, PHASES[0].chunks + RING):
                w_chunk(c, c % RING)
            sp.dma_start(tab[:, EARLY:], table_t[:, EARLY:]).then_inc(table_in, 16)

            def body(i, p, it, peeled, follow):
                for j in ahead_range(i, peeled):
                    w_chunk(ahead(i, it, j)[0], j % RING)
                    for s in ada_part(p, it, j, ADA_CHUNKS):
                        ada_chunk((0 if p.heads else it * p.ada) + (ADA0[i] + s // ADA_CHUNKS), s % ADA_CHUNKS)

            run_phases(sp, body, {}, lambda i, p: None)
            for q in range(4):
                sp.wait_ge(out_ready, q + 1)
                sp.dma_start(out_t[:, 4 * q:4 * q + 4, :], xs[:, 4 * q:4 * q + 4, :]).then_inc(out_stored, 16)
            sp.wait_ge(out_stored, 64)

        @block.scalar
        def _(act):
            def w_hi(number, uses, slot):
                act.wait_ge(raw_in[slot], uses * 16 + 16)
                act.wait_ge(w_free, number + 1)
                nc.scalar.copy(whi[:, slot, :], raw[:, slot, :]).then_inc(hi_ready, 1)

            def square(n, q, tile, step):
                if n > 0:
                    act.wait_ge(part_ready, step)
                nc.scalar.activation(s2[:, :, :], xs[:, bass.ds(tile, NT), :], ACT.Square).then_inc(sq_ready, 1)

            def take_root(n):
                act.wait_ge(mean_ready, n + 1)
                nc.scalar.activation(root[:, :], ps[:, MISC, 0:T], ACT.Sqrt, bias=eps[:, 0:1]).then_inc(root_ready, 1)

            def modulate(n, pairs):
                for j in pairs:
                    act.wait_ge(xn_ready, 8 * n + j + 1)
                    for t in range(2):
                        k = 2 * j + t
                        ins = nc.scalar.activation(xsp[:, k, 0:T], scaled(j)[:, t, :], ACT.Identity,
                                                   bias=ada[:, 3 * n * DT + k:3 * n * DT + k + 1])
                    ins.then_inc(mod_hi, 1)

            def keep_v(m):
                act.wait_ge(v_turned, m + 1)
                nc.scalar.copy(proj[:, AV + m if m < HEADS else RV + m - HEADS, :],
                               ps[:, 7, 0:T]).then_inc(v_kept, 1)

            def exp(h):
                act.wait_ge(max_ready, h + 1)
                e = att_buf(s0, h)
                nc.scalar.activation(e[:, 0:P], e[:, 0:P], ACT.Exp, bias=nmx[:, h % 2, 0:1])
                nc.scalar.activation(e[:, P:3 * P], e[:, P:3 * P], ACT.Exp, bias=nmx[:, h % 2, 1:2]).then_inc(exp_ready, 1)

            def keep_p(h):
                act.wait_ge(pt_done, h + 1)
                if h >= 2:
                    act.wait_ge(ao_done, h - 1)
                nc.scalar.copy(att_buf(s1, h), ps[:, 5, 0:3 * P]).then_inc(pt_kept, 1)

            def keep_y(h):
                act.wait_ge(ao_done, h + 1)
                nc.scalar.copy(proj[:, AQ + h, :], ps[:, 6, 0:T]).then_inc(y_att, 1)

            def keep_o(h):
                act.wait_ge(ro_done, h + 1)
                nc.scalar.copy(proj[:, RV + h, :], ps[:, 5, 0:T]).then_inc(ro_kept, 1)

            def std(half):
                act.wait_ge(var_ready, half + 1)
                c = slice(HEADS * half, HEADS * half + HEADS)
                nc.scalar.activation(var[:, 2, c], var[:, 1, c], ACT.Sqrt).then_inc(std_ready, 1)

            def silu(half):
                act.wait_ge(in_kept, SETS + IN0[HEADS_AT + 1] - 1 + half)
                g = proj[:, RG + 4 * half:RG + 4 * half + 4, :]
                nc.scalar.activation(g, g, ACT.Silu).then_inc(g_silu, 1)

            def split_hi(m):
                if m == 0:
                    act.wait_ge(w_free, RING + CHUNK0[HEADS_AT + 1])
                    act.wait_ge(y_att, HEADS)
                if m >= 4:
                    act.wait_ge(y_ret, 2 * (m - 4) + 2)
                nc.scalar.copy(xsp[:, 2 * m:2 * m + 2, 0:T], y_tiles(m)).then_inc(y_hi, 1)

            act.wait_ge(const_in, 64)
            nc.scalar.activation(cc[:, 1, :], cc[:, 0, :], ACT.Silu).then_inc(c_ready, 1)
            act.wait_ge(x_loaded, 16)
            for q in range(QUARTERS):
                if q > 0:
                    act.wait_ge(part_ready, q)
                square(0, q, NT * q, q)
            take_root(0)
            for q in range(QUARTERS):
                for c in range(4 * q, 4 * q + 4):
                    w_hi(c, c // RING, c % RING)
                modulate(0, range(2 * q, 2 * q + 2))

            def take_gate(done):
                act.wait_ge(w_free, done)
                nc.scalar.activation(s1[:, :, :], group_out(0), ACT.Silu).then_inc(silu_ready, 1)

            def hid_hi_part(i, p, it):
                act.wait_ge(hid_f32, it + (HID0[i] + 2))
                nc.scalar.copy(hid[:, bass.ds(it * NT + p.tile0, NT), 0:T], s3[:, :, :]).then_inc(hid_hi, 1)

            for c in range(PHASES[0].chunks, PHASES[0].chunks + RING):
                if c == PHASES[0].chunks + 2:
                    take_gate(RING + PHASES[0].chunks - 2)
                w_hi(c, c // RING, c % RING)
            hid_hi_part(0, PHASES[0], 0)

            def body(i, p, it, peeled, follow):
                def res_squares(g):
                    act.wait_ge(res_step, it * 2 + (SETS + RES0[i] + g + 1))
                    square(p.squares, None, it * 2 * NT + g * NT, it * 2 + (QUARTERS * p.squares + g))

                for j in ahead_range(i, peeled):
                    if p.kind == UP and j == p.group_chunks:
                        take_gate(group_end(i, it, 0))
                    if p.squares is not None and j == p.group_chunks + 1:
                        res_squares(0)
                    number, uses = ahead(i, it, j)
                    w_hi(number, uses, j % RING)
                    if follow:
                        follow(it * p.chunks + j)
                if p.kind == UP:
                    hid_hi_part(i, p, it)
                if p.squares is not None:
                    res_squares(1)

            def after(i, p):
                if p.squares is not None:
                    take_root(p.squares)
                    if p.squares < 3:
                        modulate(p.squares, range(DT // 2))

            run_phases(act, body, {"turn_v": keep_v, "exp": exp, "turn_p": keep_p, "attend": keep_y,
                                   "ret_out": keep_o, "std": std, "silu": silu, "split": split_hi}, after)

        @block.vector
        def _(dve):
            steps = [0]

            def then(ins):
                steps[0] += 1
                ins.then_inc(dve_step, 1)
                dve.wait_ge(dve_step, steps[0])

            def w_lo(number, slot):
                dve.wait_ge(hi_ready, number + 1)
                nc.vector.tensor_tensor(wlo[:, slot, :], raw[:, slot, :], whi[:, slot, :].bitcast(F32),
                                        ALU.subtract).then_inc(lo_ready, 1)

            def ada_mac(group, k, slot):
                chunk = k // KC
                src = araw[:, chunk % RING, (k % KC) * GW:(k % KC) * GW + GW]
                dst = acc[:, bass.ds(slot, 1), :].rearrange("p a n -> p (a n)")
                if k % KC == 0:
                    dve.wait_ge(ada_in[chunk % RING],
                                group * (16 * ADA_CHUNKS // RING) + (chunk // RING + 1) * 16)
                if k == 0:
                    nc.vector.tensor_scalar(dst, src, cc[:, 1, 0:1], None, ALU.mult).then_inc(ada_step, 1)
                else:
                    dve.wait_ge(ada_step, group * ADA_STEPS + (2 * RING + k))
                    nc.vector.scalar_tensor_tensor(out=dst, in0=src, scalar=cc[:, 1, k:k + 1], in1=dst,
                                                   op0=ALU.mult, op1=ALU.add).then_inc(ada_step, 1)

            def ada_keep(rnd, dst, n):
                dve.wait_ge(ada_turned, rnd + 1)
                nc.vector.tensor_reduce(asum[:, 0:n * NT], ps[:, 6:6 + n, :].rearrange("p b (n q) -> p (b n) q", q=P),
                                        AX.X, ALU.add).then_inc(asum_ready, 1)
                dve.wait_ge(asum_ready, rnd + 1)
                nc.vector.tensor_tensor(dst, asum_like(dst, n), dst, ALU.add).then_inc(ada_out, 1)

            def asum_like(dst, n):
                return asum[:, 0:n * NT] if len(dst.shape) == 2 else asum[:, 0:n * NT].rearrange(
                    "p (b n) -> p b n", b=n)

            def set_gate(layer, factor):
                c = slice((3 * layer + 2) * DT, (3 * layer + 3) * DT)
                then(nc.vector.tensor_scalar(gate[:, :], ada[:, c], factor, None, ALU.mult))

            def sum_squares(dst_q, step):
                dve.wait_ge(sq_ready, step + 1)
                nc.vector.tensor_reduce(s0[:, bass.ds(dst_q, 1), :].rearrange("p a t -> p (a t)"),
                                        s2[:, :, :].rearrange("p a t -> p t a"), AX.X, ALU.add).then_inc(part_ready, 1)

            def inverse_root(n):
                dve.wait_ge(root_ready, n + 1)
                then(nc.vector.reciprocal(rms[:, :], root[:, :]))

            def mod_scale(n, tiles, rounds):
                dve.wait_ge(ada_out, rounds)
                a = (3 * n + 1) * DT
                nc.vector.scalar_tensor_tensor(out=scl[:, tiles], in0=ada[:, a + tiles.start:a + tiles.stop], scalar=1.0,
                                               in1=gain[:, n, tiles], op0=ALU.add, op1=ALU.mult).then_inc(scl_ready, 1)

            def modulate(n, pairs):
                def lo(j):
                    dve.wait_ge(mod_hi, 8 * n + j + 1)
                    for t in range(2):
                        k = 2 * j + t
                        ins = nc.vector.scalar_tensor_tensor(
                            out=xsp[:, k, T:2 * T], in0=scaled(j)[:, t, :],
                            scalar=ada[:, 3 * n * DT + k:3 * n * DT + k + 1],
                            in1=xsp[:, k, 0:T].bitcast(F32), op0=ALU.add, op1=ALU.subtract)
                    ins.then_inc(mod_ready, 1)

                dve.wait_ge(scl_ready, pairs[0] // 2 + 1 if n == 0 else QUARTERS + n)
                for j in pairs:
                    if j >= 4:
                        dve.wait_ge(mod_ready, 8 * n + j - 3)
                    for t in range(2):
                        k = 2 * j + t
                        ins = nc.vector.scalar_tensor_tensor(out=scaled(j)[:, t, :], in0=xs[:, k, :],
                                                             scalar=scl[:, k:k + 1], in1=rms[:, :],
                                                             op0=ALU.mult, op1=ALU.mult)
                    ins.then_inc(xn_ready, 1)
                    if j > pairs[0]:
                        lo(j - 1)
                lo(pairs[-1])

            def take_group(i, p, it, g):
                if p.kind == UP and g == 0:
                    return
                dve.wait_ge(w_free, group_end(i, it, g))
                r = group_out(g)
                if p.kind == UP:
                    dve.wait_ge(silu_ready, it + (HID0[i] + 2))
                    nc.vector.tensor_tensor(s3[:, :, :], s1[:, :, :], r, ALU.mult).then_inc(hid_f32, 1)
                elif p.kind == IN:
                    nc.vector.tensor_copy(proj[:, bass.ds(it * 2 * NT + (p.tile0 + g * NT), NT), :], r).then_inc(in_kept, 1)
                else:
                    for n in range(NT):
                        tile = it * 2 * NT + (g * NT + n)
                        x = xs[:, bass.ds(tile, 1), :].rearrange("p a t -> p (a t)")
                        ins = nc.vector.scalar_tensor_tensor(out=x, in0=r[:, n, :], scalar=gate[:, bass.ds(tile, 1)],
                                                             in1=x, op0=ALU.mult, op1=ALU.add)
                    ins.then_inc(res_step, 1)

            def hid_lo(i, p, it):
                dve.wait_ge(hid_hi, it + (HID0[i] + 1))
                tiles = bass.ds(it * NT + p.tile0, NT)
                nc.vector.tensor_tensor(hid[:, tiles, T:2 * T], s3[:, :, :], hid[:, tiles, 0:T].bitcast(F32),
                                        ALU.subtract).then_inc(hid_ready, 1)

            def mask_scores(h):
                dve.wait_ge(sc_done, h + 1)
                if h >= 2:
                    dve.wait_ge(pt_done, h - 1)
                e = att_buf(s0, h)
                nc.vector.scalar_tensor_tensor(out=e, in0=ps[:, 4, 0:3 * P], scalar=ATT_SCALE, in1=mask,
                                               op0=ALU.mult, op1=ALU.add).then_inc(sc_masked, 1)
                dve.wait_ge(sc_masked, h + 1)
                nc.vector.tensor_reduce(mx[:, h % 2, 0:1], e[:, 0:P], AX.X, ALU.max)
                then(nc.vector.tensor_reduce(mx[:, h % 2, 1:2], e[:, P:3 * P], AX.X, ALU.max))
                nc.vector.tensor_scalar(nmx[:, h % 2, :], mx[:, h % 2, :], -1.0, None, ALU.mult).then_inc(max_ready, 1)

            def probs(h):
                dve.wait_ge(exp_ready, h + 1)
                e = att_buf(s0, h)
                cuts = enumerate((slice(0, P), slice(P, 3 * P)))
                for b, cut in cuts:
                    ins = nc.vector.tensor_tensor_reduce(e[:, cut], e[:, cut], count[:, cut], 1.0, 0.0, ALU.mult,
                                                         ALU.add, den[:, h % 2, b:b + 1])
                then(ins)
                then(nc.vector.reciprocal(rden[:, h % 2, :], den[:, h % 2, :]))
                for b, cut in enumerate((slice(0, P), slice(P, 3 * P))):
                    ins = nc.vector.tensor_scalar(e[:, cut], e[:, cut], rden[:, h % 2, b:b + 1], None, ALU.mult)
                ins.then_inc(p_ready, 1)

            def rotated(j):
                dve.wait_ge(rot_done, j + 1)
                if j >= 1:
                    dve.wait_ge(rot_kept, j)
                for t in range(2):
                    x = proj[:, RQ + 2 * j + t, :]
                    nc.vector.tensor_tensor(s3[:, t, :], x, cos, ALU.mult)
                    ins = nc.vector.tensor_tensor(s3[:, 2 + t, :], ps[:, 4 + j % 2, t * T:t * T + T], sin, ALU.mult)
                then(ins)
                nc.vector.tensor_tensor(proj[:, RQ + 2 * j:RQ + 2 * j + 2, :], s3[:, 0:2, :], s3[:, 2:4, :],
                                        ALU.add).then_inc(rot_kept, 1)

            def decayed(h):
                dve.wait_ge(ra_done, h + 1)
                if h >= 2:
                    dve.wait_ge(ro_done, h - 1)
                a, dec = att_buf(s2, h), tb["decay"][:, h * T:h * T + T]
                nc.vector.tensor_tensor(a[:, 0:T], ps[:, 4, 0:T], dec, ALU.mult)
                nc.vector.tensor_tensor(a[:, T:T + P], ps[:, 4, T:T + P], dec[:, 0:P], ALU.mult).then_inc(ra_kept, 1)

            def head_stats(h):
                dve.wait_ge(ro_kept, h + 1)
                nc.vector.bn_stats(stats[:, 0, :], proj[:, RV + h, 0:P])
                then(nc.vector.bn_stats(stats[:, 1, :], proj[:, RV + h, P:T]))
                nc.vector.bn_aggr(mv[:, 2 * h, :], stats[:, 0, :])
                then(nc.vector.bn_aggr(mv[:, 2 * h + 1, :], stats[:, 1, :]))

            def inverse_var(half):
                c = slice(HEADS * half, HEADS * half + HEADS)
                then(nc.vector.tensor_scalar(var[:, 0, c], mv[:, c, 1], EPS, None, ALU.add))
                nc.vector.reciprocal(var[:, 1, c], var[:, 0, c]).then_inc(var_ready, 1)

            def norm_o(h):
                dve.wait_ge(std_ready, h // 4 + 1)
                for t in range(2):
                    o, m = proj[:, RV + h, t * P:t * P + P], 2 * h + t
                    ins = nc.vector.tensor_scalar(o, o, mv[:, m, 0:1], var[:, 2, m:m + 1], ALU.subtract, ALU.mult)
                ins.then_inc(ro_norm, 1)

            def gated(h):
                dve.wait_ge(rt_done, h + 1)
                dve.wait_ge(g_silu, h // 4 + 1)
                g = proj[:, RG + h, :]
                nc.vector.tensor_tensor(g, ps[:, turn_bank(h), 0:T], g, ALU.mult).then_inc(y_ret, 1)

            def heads_ada(n):
                group = ADA0[HEADS_AT] + n
                ada_keep(ROUND0[HEADS_AT] + n, ada[:, group * NT:(group + 1) * NT], 1)

            def split_lo(m):
                dve.wait_ge(y_hi, m + 1)
                nc.vector.tensor_tensor(xsp[:, 2 * m:2 * m + 2, T:2 * T], y_tiles(m),
                                        xsp[:, 2 * m:2 * m + 2, 0:T].bitcast(F32), ALU.subtract).then_inc(y_ready, 1)

            nc.vector.memset(credit[:, 0:1], 0.0).then_inc(lo_ready, RING)
            nc.vector.memset(credit[:, 1:2], 0.0).then_inc(w_free, RING)
            nc.vector.memset(credit[:, 2:3], 0.0).then_inc(ada_step, 2 * RING)
            nc.vector.memset(credit[:, 3:4], 0.0).then_inc(in_kept, SETS)
            nc.vector.memset(credit[:, 4:5], 0.0).then_inc(res_step, SETS)
            nc.vector.memset(credit[:, 5:6], 0.0).then_inc(silu_ready, 1)
            nc.vector.memset(credit[:, 6:7], 0.0).then_inc(hid_f32, 1)
            dve.wait_ge(c_ready, 1)
            for q in range(QUARTERS):
                for n in range(2 * q, 2 * q + 2):
                    for k in range(ADA_STEPS):
                        ada_mac(n, k, n % 2)
                    if n == 0:
                        for r in range(QUARTERS):
                            sum_squares(r, r)
                        inverse_root(0)
                for c in range(4 * q, 4 * q + 4):
                    w_lo(c, c % RING)
                ada_keep(q, ada[:, 0:2 * DT].rearrange("p (v m) -> p v m", v=2)[:, :, NT * q:NT * q + NT], 2)
                mod_scale(0, slice(NT * q, NT * q + NT), q + 1)
                modulate(0, range(2 * q, 2 * q + 2))
            for c in range(PHASES[0].chunks, PHASES[0].chunks + RING):
                w_lo(c, c % RING)
            take_group(0, PHASES[0], 0, 1)
            hid_lo(0, PHASES[0], 0)

            def body(i, p, it, peeled, follow):
                def res_squares(g):
                    sum_squares(it * 2 + g, it * 2 + (QUARTERS * p.squares + g))

                for j in ahead_range(i, peeled):
                    if j == p.group_chunks:
                        take_group(i, p, it, 0)
                    w_lo(ahead(i, it, j)[0], j % RING)
                    if p.squares is not None and j == p.group_chunks + 2:
                        res_squares(0)
                    for s in ada_part(p, it, j, ADA_STEPS):
                        if p.heads:
                            n = s // ADA_STEPS
                            ada_mac(ADA0[i] + n, s % ADA_STEPS, n % ACC)
                        else:
                            ada_mac(it * p.ada + (ADA0[i] + s // ADA_STEPS), s % ADA_STEPS, s // ADA_STEPS)
                    if follow:
                        follow(it * p.chunks + j)
                take_group(i, p, it, 1)
                if p.kind == UP:
                    hid_lo(i, p, it)
                if p.squares is not None:
                    res_squares(1)
                if p.ada and not p.heads:
                    ada_keep(it + ROUND0[i], ada[:, bass.ds(it * (p.ada * NT) + ADA0[i] * NT, p.ada * NT)], p.ada)

            def after(i, p):
                if i in GATE_AFTER:
                    dve.wait_ge(ada_out, ROUND0[i + 1])
                    set_gate(*GATE_AFTER[i])
                if p.squares is not None:
                    if p.squares < 3:
                        mod_scale(p.squares, slice(0, DT), ROUND0[i + 1])
                    inverse_root(p.squares)
                    if p.squares < 3:
                        modulate(p.squares, range(DT // 2))

            run_phases(dve, body, {"mask": mask_scores, "probs": probs, "rotate": rotated, "ret_scores": decayed,
                                   "stats": head_stats, "std": inverse_var, "norm_o": norm_o, "gate": gated,
                                   "split": split_lo, "ada": heads_ada}, after)
            for k in range(DT):
                ins = nc.vector.scalar_tensor_tensor(out=xs[:, k, :], in0=xs[:, k, :], scalar=gain[:, 3, k:k + 1],
                                                     in1=rms[:, :], op0=ALU.mult, op1=ALU.mult)
                if k % 4 == 3:
                    ins.then_inc(out_ready, 1)

        @block.tensor
        def _(pe):
            def group_chunk(slot, x, k0, bank, last_k):
                for k in range(k0, k0 + KC):
                    for n in range(NT):
                        at = (k - k0) * GW + n * P
                        o = ps[:, bank + n // 2, (n % 2) * T:(n % 2) * T + T]
                        hi, lo = whi[:, slot, at:at + P], wlo[:, slot, at:at + P]
                        nc.tensor.matmul(o, hi, x[:, k, 0:T], start=(k == 0 and n % 2 == 0), stop=False,
                                         skip_group_check=True)
                        nc.tensor.matmul(o, hi, x[:, k, T:2 * T], start=False, stop=False, skip_group_check=True)
                        ins = nc.tensor.matmul(o, lo, x[:, k, 0:T], start=False, stop=(k == last_k),
                                               skip_group_check=True)
                return ins

            def ada_turn(rnd, total, n, first=0):
                pe.wait_ge(ada_step, total * ADA_STEPS + 2 * RING)
                if rnd is not None:
                    pe.wait_ge(ada_out, rnd)
                for m in range(n):
                    for t in range(NT):
                        ins = nc.tensor.transpose(ps[:, 6 + m, t * P:t * P + P], acc[:, first + m, t * P:t * P + P], ident)
                ins.then_inc(ada_turned, 1)

            def mean(n):
                for q in range(QUARTERS):
                    pe.wait_ge(part_ready, QUARTERS * n + q + 1)
                    ins = nc.tensor.matmul(ps[:, MISC, 0:T], ones_mean, s0[:, q, :], start=(q == 0),
                                           stop=(q == QUARTERS - 1))
                ins.then_inc(mean_ready, 1)

            def turn_v(m):
                if m >= HEADS:
                    pe.wait_ge(in_kept, SETS + IN0[HEADS_AT] + 3 + (m - HEADS) // 4)
                if m >= 1:
                    pe.wait_ge(v_kept, m)
                v = proj[:, AV + m if m < HEADS else RV + m - HEADS, :]
                for t in range(2):
                    ins = nc.tensor.transpose(ps[:, 7, t * P:t * P + P], v[:, t * P:t * P + P], ident)
                ins.then_inc(v_turned, 1)

            def scores(h):
                if h == 0:
                    pe.wait_ge(table_in, 16)
                pe.wait_ge(in_kept, SETS + IN0[HEADS_AT])
                if h >= 1:
                    pe.wait_ge(sc_masked, h)
                q, k = proj[:, AQ + h, :], proj[:, AK + h, :]
                nc.tensor.matmul(ps[:, 4, 0:P], q[:, 0:P], k[:, 0:P], start=True, stop=True)
                nc.tensor.matmul(ps[:, 4, P:3 * P], q[:, P:T], k, start=True, stop=True).then_inc(sc_done, 1)

            def turn_p(h):
                pe.wait_ge(p_ready, h + 1)
                if h >= 1:
                    pe.wait_ge(pt_kept, h)
                e = att_buf(s0, h)
                for b in range(3):
                    ins = nc.tensor.transpose(ps[:, 5, b * P:b * P + P], e[:, b * P:b * P + P], ident)
                ins.then_inc(pt_done, 1)

            def attend(h):
                pe.wait_ge(pt_kept, h + 1)
                pe.wait_ge(v_kept, h + 1)
                if h >= 1:
                    pe.wait_ge(y_att, h)
                pt, v = att_buf(s1, h), proj[:, AV + h, :]
                nc.tensor.matmul(ps[:, 6, 0:T], v[:, 0:P], pt[:, 0:T], start=True, stop=False, skip_group_check=True)
                nc.tensor.matmul(ps[:, 6, P:T], v[:, P:T], pt[:, T:T + P], start=False, stop=True,
                                 skip_group_check=True).then_inc(ao_done, 1)

            def rotate_pair(j):
                pe.wait_ge(in_kept, SETS + IN0[HEADS_AT] + 2)
                if j == 0:
                    pe.wait_ge(sc_masked, HEADS)
                elif j == 1:
                    pe.wait_ge(pt_kept, HEADS)
                else:
                    pe.wait_ge(rot_kept, j - 1)
                x = proj[:, RQ + 2 * j:RQ + 2 * j + 2, :].rearrange("p a t -> p (a t)")
                nc.tensor.matmul(ps[:, 4 + j % 2, :], rotate, x, start=True, stop=True).then_inc(rot_done, 1)

            def ret_scores(h):
                pe.wait_ge(rot_kept, 4)
                if h >= 1:
                    pe.wait_ge(ra_kept, h)
                rows = slice(DK * (h % 2), DK * (h % 2) + DK)
                q, k = proj[rows, RQ + h // 2, :], proj[rows, RK + h // 2, :]
                nc.tensor.matmul(ps[:, 4, 0:T], k[:, 0:P], q, start=True, stop=True)
                nc.tensor.matmul(ps[:, 4, T:T + P], k[:, P:T], q[:, P:T], start=True, stop=True).then_inc(ra_done, 1)

            def ret_out(h):
                pe.wait_ge(ra_kept, h + 1)
                pe.wait_ge(v_kept, HEADS + h + 1)
                if h >= 1:
                    pe.wait_ge(ro_kept, h)
                a, v = att_buf(s2, h), proj[:, RV + h, :]
                nc.tensor.matmul(ps[:, 5, 0:P], a[:, 0:P], v[:, 0:P], start=True, stop=True)
                nc.tensor.matmul(ps[:, 5, P:T], a[:, P:T], v[:, 0:P], start=True, stop=False)
                nc.tensor.matmul(ps[:, 5, P:T], a[:, T:T + P], v[:, P:T], start=False, stop=True).then_inc(ro_done, 1)

            def turn_o(h):
                pe.wait_ge(ro_norm, h + 1)
                if h == 0:
                    pe.wait_ge(v_kept, 2 * HEADS)
                elif h < 4:
                    pe.wait_ge(y_ret, h)
                else:
                    pe.wait_ge(*[(ra_kept, HEADS), (ro_kept, HEADS), (ada_out, ROUND0[HEADS_AT + 1]), (y_ret, 4)][h - 4])
                for t in range(2):
                    ins = nc.tensor.transpose(ps[:, turn_bank(h), t * P:t * P + P],
                                              proj[:, RV + h, t * P:t * P + P], ident)
                ins.then_inc(rt_done, 1)

            def heads_ada(n):
                pe.wait_ge(y_att, HEADS)
                ada_turn(ROUND0[HEADS_AT] + n, ADA0[HEADS_AT] + n + 1, 1, n % ACC)

            pe.wait_ge(const_in, 64)
            mean(0)
            for q in range(QUARTERS):
                ada_turn(q if q else None, 2 * q + 2, 2)
                for c in range(4 * q, 4 * q + 4):
                    g, k0 = c % 4 // 2, NT * q + KC * (c % 2)
                    pe.wait_ge(lo_ready, RING + c + 1)
                    pe.wait_ge(mod_ready, k0 // 2 + 1)
                    group_chunk(c % RING, xsp, k0, 2 * g, DT - 1).then_inc(w_free, 1)

            def set_out(i, bodies, g):
                if PHASES[i].kind == UP:
                    pe.wait_ge(hid_f32 if g else silu_ready, bodies + (HID0[i] + 1))
                elif PHASES[i].kind == IN:
                    pe.wait_ge(in_kept, bodies * 2 + (SETS - 1 + g + IN0[i]))
                else:
                    pe.wait_ge(res_step, bodies * 2 + (SETS - 1 + g + RES0[i]))

            def body(i, p, it, peeled, follow):
                x = hid if p.kind == DOWN else xsp
                for g in range(2):
                    if i > 0:
                        set_out(i - 1, PHASES[i - 1].bodies, g)
                    set_out(i, it, g)
                    for j in range(p.group_chunks):
                        c = g * p.group_chunks + j
                        pe.wait_ge(lo_ready, it * p.chunks + (RING + CHUNK0[i] + c + 1))
                        if p.norm is not None and g == 0:
                            pe.wait_ge(mod_ready, 8 * p.norm + j + 1)
                        if p.kind == OUT and g == 0:
                            pe.wait_ge(y_ready, j + 1)
                        if p.kind == DOWN and g == 0 and j in (0, p.group_chunks - 2):
                            pe.wait_ge(hid_ready, HID0[i] - (j == 0))
                        group_chunk(c % RING, x, KC * j, 2 * g, KC * p.group_chunks - 1).then_inc(w_free, 1)
                        if follow:
                            follow(it * p.chunks + c)
                if p.ada and not p.heads:
                    ada_turn(it + ROUND0[i], it * p.ada + (ADA0[i] + p.ada), p.ada)

            def after(i, p):
                if p.squares is not None:
                    mean(p.squares)

            def run():
                for i, p in enumerate(PHASES):
                    if p.heads:
                        def follow(chunk):
                            for name, n in SCHEDULE.get(chunk, ()):
                                if name in stage:
                                    stage[name](n)

                        for it in range(p.bodies):
                            body(i, p, it, False, follow)
                        follow(p.chunks * p.bodies)
                    elif i > 0:
                        with pe.Fori(0, p.bodies) as it:
                            body(i, p, it, False, None)
                    after(i, p)

            stage = {"turn_v": turn_v, "scores": scores, "turn_p": turn_p, "attend": attend, "rotate": rotate_pair,
                     "ret_scores": ret_scores, "ret_out": ret_out, "turn_o": turn_o, "ada": heads_ada}
            run()


def chunks(w):
    k, n = w.shape
    return w.reshape(k // (KC * P), KC, P, n // GW, GW).transpose(3, 0, 2, 1, 4).reshape(n // GW, k // (KC * P), P, CH)


def columns(v):
    return np.ascontiguousarray(v.reshape(-1, P).T)


def weights_in_order(w1_gate, w1_up, w1_down, w_in, w_out, w2_gate, w2_up, w2_down):
    total = sum(p.chunks * p.bodies for p in PHASES)
    flat = np.empty((total, P, CH), np.float32)
    at = 0

    def put(part):
        nonlocal at
        part = part.reshape(-1, P, CH)
        flat[at:at + len(part)] = part
        at += len(part)

    def swiglu(gate, up, down):
        gate, up, down = chunks(gate), chunks(up), chunks(down)
        cut = FA * NT // KC
        for first, last in ((0, FA), (FA, FA + FB)):
            for g in range(first, last):
                both = np.stack([gate[g], up[g]])
                if at == 0:
                    both = both.reshape(2, QUARTERS, 2, P, CH).transpose(1, 0, 2, 3, 4)
                put(both)
            put(down[:, :cut] if first == 0 else down[:, cut:])

    swiglu(w1_gate, w1_up, w1_down)
    put(chunks(w_in))
    put(chunks(w_out))
    swiglu(w2_gate, w2_up, w2_down)
    return flat


def kernel(x, c, w_ada, b_ada, g_ffn1, w1_gate, w1_up, w1_down, g_mix, w_in, w_out,
           g_ffn2, w2_gate, w2_up, w2_down, g_final):
    import concourse.bacc as _bacc
    from concourse.bass_utils import run_bass_kernel_spmd as _run

    nc = _bacc.Bacc("TRN2", target_bir_lowering=False, num_devices=1)
    arrays = {
        "x_t": np.ascontiguousarray(x[0].T.reshape(DT, P, T).transpose(1, 0, 2)),
        "c_t": columns(c[0]),
        "w_ada_chunks": chunks(w_ada[0])[ADA_ORDER].reshape(-1, P, CH),
        "b_ada_t": columns(b_ada[0]),
        "gains_t": np.stack([columns(g_ffn1[0]), columns(g_mix[0]), columns(g_ffn2[0]), columns(g_final)], 1),
        "w_chunks": weights_in_order(w1_gate[0], w1_up[0], w1_down[0], w_in[0], w_out[0], w2_gate[0], w2_up[0],
                                     w2_down[0]),
        "tables": tables(),
    }
    args = [nc.dram_tensor(name, a.shape, F32, kind="ExternalInput").ap() for name, a in arrays.items()]
    out = nc.dram_tensor("out_t", (P, DT, T), F32, kind="ExternalOutput").ap()
    build(nc, *args, out)
    r = _run(nc, [arrays], core_ids=[0])
    got = r.results[0]["out_t"]
    return np.ascontiguousarray(got.transpose(1, 0, 2).reshape(D, T).T)[None]
```

```python
from contextlib import ExitStack

import numpy as np
import concourse.bass as bass
import concourse.mybir as mybir

F32 = mybir.dt.float32
F32R = mybir.dt.float32r
ALU = mybir.AluOpType
ACT = mybir.ActivationFunctionType
AX = mybir.AxisListType

P = 128
T = 256
D = 2048
DT = D // P
FF = 5632
GW = 512
NT = GW // P
KC = 2
CH = KC * GW
RING = 4
SETS = 2
HEADS = 8
DH = 128
DK = 64
MIX_IN = 6144
EPS = 1e-6
ATT_SCALE = DH ** -0.5
RET_SCALE = DK ** -0.5
NEG = -1.0e30
FA = 6
FB = FF // GW - FA
ADA_CHUNKS = DT // KC
ADA_STEPS = DT
EARLY_RING = 12
ACC = 2
ADA_REST = 2
HEADS_ADA = (27, 30, 43)
ROTATE_AT = (11, 12, 14, 15, 17, 18, 20, 21)
RET_CHUNK = 26
AQ, AK, AV, RQ, RK, RV, RG = 0, 8, 16, 24, 28, 32, 40


class Phase:

    def __init__(self, kind, bodies, kt, ada=0, norm=None, tile0=0, squares=None, heads=False):
        self.kind, self.bodies, self.ada, self.norm = kind, bodies, ada, norm
        self.tile0, self.squares, self.heads = tile0, squares, heads
        self.group_chunks = kt // KC
        self.chunks = 2 * self.group_chunks
        self.rounds = (ada if heads else bodies) if ada else 0


UP, DOWN, IN, OUT = "up", "down", "in", "out"
PHASES = [
    Phase(UP, 1, DT, norm=0),
    Phase(UP, FA - 1, DT, ada=1, tile0=NT),
    Phase(DOWN, 2, FA * NT, ada=2),
    Phase(UP, FB, DT, ada=1),
    Phase(DOWN, 2, FB * NT, ada=1, squares=1),
    Phase(IN, 3, DT, ada=1, norm=1),
    Phase(IN, 3, DT, ada=3, tile0=RQ, heads=True),
    Phase(OUT, 2, DT, ada=1, squares=2),
    Phase(UP, 4, DT, ada=1, norm=2),
    Phase(UP, FA - 4, DT, tile0=4 * NT),
    Phase(DOWN, 2, FA * NT),
    Phase(UP, FB, DT),
    Phase(DOWN, 2, FB * NT, squares=3),
]
GATE_AFTER = {1: (0, 0.5), 6: (1, 1.0), 8: (2, 0.5)}
QUARTERS = DT // NT
ADA_FIRST = 2 * QUARTERS
ADA_ORDER = [q + QUARTERS * v for q in range(QUARTERS) for v in range(2)] + list(range(ADA_FIRST, 9 * D // GW))


def plan():
    rows, c, a, h, r, n, rnd = [], 0, ADA_FIRST, 0, 0, 0, QUARTERS
    for p in PHASES:
        rows.append((c, a, h, r, n, rnd))
        c += p.chunks * p.bodies
        a += p.ada * (1 if p.heads else p.bodies)
        h += p.bodies if p.kind == UP else 0
        r += 2 * p.bodies if p.kind in (DOWN, OUT) else 0
        n += 2 * p.bodies if p.kind == IN else 0
        rnd += p.rounds
    rows.append((c, a, h, r, n, rnd))
    return [list(x) for x in zip(*rows)]


CHUNK0, ADA0, HID0, RES0, IN0, ROUND0 = plan()
assert ADA0[-1] == 9 * D // GW and all(p.chunks % RING == 0 for p in PHASES)
HEADS_AT = next(i for i, p in enumerate(PHASES) if p.heads)


def head_schedule():
    table = {}

    def put(chunk, *stages):
        table.setdefault(chunk, []).extend(stages)

    for h in range(HEADS):
        put(3 * h, ("turn_v", h), ("scores", h), ("mask", h))
        put(3 * h + 1, ("exp", h))
        put(3 * h + 2, ("probs", h))
        put(3 * h + 3, ("turn_p", h))
        put(3 * h + 4, ("attend", h), ("split_att", h))
    for j, chunk in enumerate(ROTATE_AT):
        put(chunk, ("rotate", j))
    for j in range(4):
        put(25 + j, ("turn_v", HEADS + j))
        put(33 + j, ("turn_v", HEADS + 4 + j))
    for n, chunk in enumerate(HEADS_ADA):
        put(chunk, ("ada", n))
    for h in range(HEADS):
        put(RET_CHUNK + 2 * h, ("ret_scores", h))
        put(RET_CHUNK + 2 * h + 1, ("ret_out", h))
        put(RET_CHUNK + 2 * h + 2, ("stats", h))
    put(36, ("std", 0))
    for h in range(4):
        put(37 + h, ("norm_o", h))
    put(41, ("silu", 0), ("turn_o", 0), ("turn_o", 1))
    put(42, ("gate", 0), ("gate", 1))
    put(43, ("std", 1), ("turn_o", 2), ("turn_o", 3), ("split_ret", 0), ("split_ret", 1))
    put(44, *[("norm_o", h) for h in range(4, 8)], ("gate", 2), ("gate", 3))
    put(45, ("split_ret", 2), ("split_ret", 3), ("turn_o", 4), ("turn_o", 5))
    put(46, ("turn_o", 6), ("turn_o", 7))
    put(48, ("silu", 1), *[("gate", h) for h in range(4, 8)], *[("split_ret", h) for h in range(4, 8)])
    return table


SCHEDULE = head_schedule()


TABLE = [("ident", P), ("ones_mean", P), ("eps", 2), ("rotate", P), ("cos", T), ("sin", T),
         ("mask", 3 * P), ("count", 3 * P), ("decay", HEADS * T)]


def tables():
    i = np.arange(P)
    part = {"ident": np.eye(P), "ones_mean": np.full((P, P), 1.0 / D), "eps": np.full((P, 2), EPS)}
    rotate = np.zeros((P, P))
    rotate[i[1::2], i[0::2]] = -1.0
    rotate[i[0::2], i[1::2]] = 1.0
    part["rotate"] = rotate
    angle = np.repeat(np.float32(1.0) / (np.float32(10000.0) ** np.linspace(0, 1, DK // 2, dtype=np.float32)), 2)
    theta = (angle[i % DK][:, None] * np.arange(T, dtype=np.float32)[None, :]).astype(np.float64)
    part["cos"], part["sin"] = np.cos(theta), np.sin(theta)
    dist = np.concatenate([i[:, None] - i[None, :], i[:, None] + P - i[None, :], i[:, None] - i[None, :]], 1)
    count = sum(((dist >= 0) & (dist <= window) & (dist % dilation == 0)).astype(float)
                for window, dilation in ((128, 1), (512, 4), (2048, 16)))
    part["mask"], part["count"] = np.where(count > 0, 0.0, NEG), count
    far = np.arange(T)[None, :] - i[:, None]
    log_g = np.log(1.0 - 2.0 ** (-5.0 - np.arange(HEADS)))
    part["decay"] = np.concatenate(
        [np.where(far >= 0, np.exp(np.maximum(far, 0) * lg) * RET_SCALE, 0.0) for lg in log_g], 1)
    return np.concatenate([part[n] for n, _ in TABLE], 1).astype(np.float32)


EARLY = sum(n for _, n in TABLE[:3])


def build(nc, x_in_t, c_in_t, w_ada, b_ada_t, gains_t, w_all, table_t, out_t):
    with ExitStack() as ctx:
        def sb(name, shape, dt=F32):
            return ctx.enter_context(nc.sbuf_tensor(name, shape, dt))

        def sem(name):
            return ctx.enter_context(nc.semaphore(name))

        xs = sb("residual", [P, DT, T])
        xsp = sb("x_split", [P, DT, 2 * T], F32R)
        raw = sb("w_raw", [P, RING, CH])
        whi = sb("w_hi", [P, RING, CH], F32R)
        wlo = sb("w_lo", [P, RING, CH], F32R)
        araw = sb("ada_raw", [P, RING, CH])
        acc = sb("ada_acc", [P, ACC, GW])
        s0 = sb("scratch0", [P, NT, T])
        s1 = sb("scratch1", [P, NT, T])
        s2 = sb("scratch2", [P, NT, T])
        s3 = sb("scratch3", [P, NT, T])
        tab = sb("table", [P, table_t.shape[1]])
        ada = sb("ada", [P, 9 * DT])
        gain = sb("gains", [P, 4, DT])
        scl = sb("mod_scale", [P, DT])
        gate = sb("res_gate", [P, DT])
        cc = sb("cond", [P, 2, DT])
        credit = sb("credit", [P, 7])
        asum = sb("ada_sums", [P, ACC * NT])
        root = sb("root", [P, T])
        rms = sb("rms", [P, T])
        var = sb("var", [P, 3, 2 * HEADS])
        mv = sb("mean_var", [P, 2 * HEADS, 2])
        stats = sb("stats", [P, 2, 6])
        mx = sb("score_max", [P, 2, 2])
        nmx = sb("neg_max", [P, 2, 2])
        den = sb("den", [P, 2, 2])
        rden = sb("rden", [P, 2, 2])
        HID_BYTES = FA * NT * 2 * T * 4
        assert HID_BYTES == (MIX_IN // P) * T * 4
        top = (nc.sbuf_usable_end - HID_BYTES) // 32 * 32
        assert nc.sbuf_base <= top, (nc.sbuf_base, top)
        hid = nc.alloc_sbuf_tensor_at("hidden", [P, FA * NT, 2 * T], F32R, offset=top)
        proj = nc.alloc_sbuf_tensor_at("projections", [P, MIX_IN // P, T], F32, offset=top)
        proj_r = nc.alloc_sbuf_tensor_at("projections_split", [P, MIX_IN // P, T], F32R, offset=top)
        assert EARLY_RING * CH * 4 <= HID_BYTES
        ada_early = nc.alloc_sbuf_tensor_at("ada_early", [P, EARLY_RING, CH], F32, offset=top)
        ps = ctx.enter_context(nc.psum_tensor("banks", [P, 8, 512], F32))

        tb, at = {}, 0
        for name, n in TABLE:
            tb[name] = tab[:, at:at + n]
            at += n
        ident, ones_mean, eps, rotate = tb["ident"], tb["ones_mean"], tb["eps"], tb["rotate"]
        cos, sin, mask, count = tb["cos"], tb["sin"], tb["mask"], tb["count"]

        const_in = sem("const_in")
        table_in = sem("table_in")
        x_loaded = sem("x_loaded")
        raw_in = [sem(f"raw_in{i}") for i in range(RING)]
        ada_in = [sem(f"ada_in{i}") for i in range(RING)]
        early_in = [sem(f"early_in{i}") for i in range(EARLY_RING)]
        hi_ready = sem("hi_ready")
        lo_ready = sem("lo_ready")
        w_free = sem("w_free")
        ada_step = sem("ada_step")
        ada_used = sem("ada_used")
        ada_merged = sem("ada_merged")
        in_kept = sem("in_kept")
        silu_ready = sem("silu_ready")
        hid_f32 = sem("hid_f32")
        hid_hi = sem("hid_hi")
        hid_ready = sem("hid_ready")
        res_step = sem("res_step")
        c_ready = sem("c_ready")
        ada_turned = sem("ada_turned")
        asum_ready = sem("asum_ready")
        ada_out = sem("ada_out")
        sq_ready = sem("sq_ready")
        part_ready = sem("part_ready")
        mean_ready = sem("mean_ready")
        root_ready = sem("root_ready")
        scl_ready = sem("scl_ready")
        xn_ready = sem("xn_ready")
        mod_hi = sem("mod_hi")
        mod_ready = sem("mod_ready")
        dve_step = sem("dve_step")
        v_turned = sem("v_turned")
        v_kept = sem("v_kept")
        g_silu = sem("g_silu")
        rot_done = sem("rot_done")
        rot_kept = sem("rot_kept")
        ra_done = sem("ra_done")
        ra_kept = sem("ra_kept")
        ro_done = sem("ro_done")
        ro_kept = sem("ro_kept")
        var_ready = sem("var_ready")
        std_ready = sem("std_ready")
        ro_norm = sem("ro_norm")
        rt_done = sem("rt_done")
        y_ret = sem("y_ret")
        y_hi = sem("y_hi")
        y_ready = sem("y_ready")
        sc_done = sem("sc_done")
        sc_masked = sem("sc_masked")
        max_ready = sem("max_ready")
        exp_ready = sem("exp_ready")
        p_ready = sem("p_ready")
        pt_done = sem("pt_done")
        pt_kept = sem("pt_kept")
        ao_done = sem("ao_done")
        out_ready = sem("out_ready")
        out_stored = sem("out_stored")

        block = ctx.enter_context(nc.Block())

        MISC = 4

        def group_out(g):
            return ps[:, 2 * g:2 * g + 2, :].rearrange("p b (n t) -> p (b n) t", t=T)

        def ahead_range(i, peeled):
            return range(PHASES[i].chunks - (RING if peeled else 0))

        def ahead(i, it, j):
            p = PHASES[i]
            return (it * p.chunks + (CHUNK0[i] + RING + j),
                    it * (p.chunks // RING) + (CHUNK0[i] + RING + j) // RING)

        def turned_o(h):
            return ps[:, 7 if h < 4 else 4 + (h - 4) // 2, h % 2 * T:h % 2 * T + T]

        def y_split(k):
            hi, lo = (AQ + k, AK + k) if k < HEADS else (RV + k - HEADS, RG + k - HEADS)
            return proj_r[:, hi, :], proj_r[:, lo, :]

        def row_bank(n):
            return 5 if n % 2 == 0 else 7

        def scaled(j):
            return (s2, s3)[j // 2 % 2][:, 2 * (j % 2):2 * (j % 2) + 2, :]

        def group_end(i, it, g):
            p = PHASES[i]
            return it * p.chunks + (RING + CHUNK0[i] + (g + 1) * p.group_chunks)

        def spread(total, j, n):
            return range(total * j // n, total * (j + 1) // n)

        def att_buf(s, h):
            flat = s[:, :, :].rearrange("p a t -> p (a t)")
            return flat[:, (h % 2) * 512:(h % 2) * 512 + 3 * P]

        def run_phases(eng, body, stage, after, peel=True):
            for i, p in enumerate(PHASES):
                last = peel and i == len(PHASES) - 1
                if p.heads:
                    def follow(chunk):
                        for name, n in SCHEDULE.get(chunk, ()):
                            if name in stage:
                                stage[name](n)

                    for it in range(p.bodies):
                        body(i, p, it, False, follow)
                    follow(p.chunks * p.bodies)
                elif i > 0:
                    with eng.Fori(0, p.bodies - 1 if last else p.bodies) as it:
                        body(i, p, it, False, None)
                    if last:
                        body(i, p, p.bodies - 1, True, None)
                after(i, p)

        def ada_part(p, it, j, total):
            if p.heads:
                j, n = it * p.chunks + j, HEADS_ADA[-1] - 1
            else:
                n = p.chunks - ADA_REST
            return spread(p.ada * total, j, n) if j < n else ()

        @block.sync
        def _(sp):
            def ada_chunk(group, k):
                sp.wait_ge(ada_step, group * ADA_STEPS + 2 * (k + 1))
                sp.dma_start(araw[:, k % RING, :], w_ada[bass.ds(group * ADA_CHUNKS + k, 1), :, :]
                             .rearrange("a p n -> (a p) n")).then_inc(ada_in[k % RING], 16)

            def w_chunk(number, slot):
                sp.wait_ge(lo_ready, number + 1)
                sp.dma_start(raw[:, slot, :], w_all[bass.ds(number, 1), :, :]
                             .rearrange("a p n -> (a p) n")).then_inc(raw_in[slot], 16)

            sp.dma_start(cc[:, 0, :], c_in_t).then_inc(const_in, 16)
            sp.dma_start(ada[:, :], b_ada_t).then_inc(const_in, 16)
            sp.dma_start(gain[:, :, :], gains_t).then_inc(const_in, 16)
            sp.dma_start(tab[:, 0:EARLY], table_t[:, 0:EARLY]).then_inc(const_in, 16)
            for q in range(QUARTERS):
                for n in range(2 * q, 2 * q + 2):
                    for k in range(ADA_CHUNKS):
                        number = ADA_CHUNKS * n + k
                        slot, before = number % EARLY_RING, number - EARLY_RING
                        if before >= 0 and k % 2 == 0:
                            sp.wait_ge(ada_step, 2 * RING + 2 * (before + 2))
                        elif before >= 0:
                            sp.wait_ge(ada_used, before // 2 + 1)
                        sp.dma_start(ada_early[:, slot, :], w_ada[number]).then_inc(early_in[slot], 16)
                        if n == 0 and k == RING - 1:
                            sp.dma_start(xs[:, :, :], x_in_t).then_inc(x_loaded, 16)
                        if (n, k) == ((1, ADA_CHUNKS - 1) if q == 0 else (2 * q, RING - 1)):
                            for c in range(4 * q, 4 * q + 4):
                                w_chunk(c, c % RING)
            for c in range(PHASES[0].chunks, PHASES[0].chunks + RING):
                w_chunk(c, c % RING)
            sp.dma_start(tab[:, EARLY:], table_t[:, EARLY:]).then_inc(table_in, 16)

            def body(i, p, it, peeled, follow):
                for j in ahead_range(i, peeled):
                    w_chunk(ahead(i, it, j)[0], j % RING)
                    for s in ada_part(p, it, j, ADA_CHUNKS):
                        ada_chunk((0 if p.heads else it * p.ada) + (ADA0[i] + s // ADA_CHUNKS), s % ADA_CHUNKS)

            run_phases(sp, body, {}, lambda i, p: None)
            for q in range(QUARTERS):
                sp.wait_ge(out_ready, q + 1)
                sp.dma_start(out_t[:, 4 * q:4 * q + 4, :], xs[:, 4 * q:4 * q + 4, :]).then_inc(out_stored, 16)
            sp.wait_ge(out_stored, 64)

        @block.scalar
        def _(act):
            def w_hi(number, uses, slot):
                act.wait_ge(raw_in[slot], uses * 16 + 16)
                act.wait_ge(w_free, number + 1)
                nc.scalar.copy(whi[:, slot, :], raw[:, slot, :]).then_inc(hi_ready, 1)

            def square(n, tile, step):
                if n > 0:
                    act.wait_ge(part_ready, step)
                nc.scalar.activation(s2[:, :, :], xs[:, bass.ds(tile, NT), :], ACT.Square).then_inc(sq_ready, 1)

            def take_root(n):
                act.wait_ge(mean_ready, n + 1)
                nc.scalar.activation(root[:, :], ps[:, MISC, 0:T], ACT.Sqrt, bias=eps[:, 0:1]).then_inc(root_ready, 1)

            def modulate(n, pairs):
                for j in pairs:
                    act.wait_ge(xn_ready, 8 * n + j + 1)
                    for t in range(2):
                        k = 2 * j + t
                        ins = nc.scalar.activation(xsp[:, k, 0:T], scaled(j)[:, t, :], ACT.Identity,
                                                   bias=ada[:, 3 * n * DT + k:3 * n * DT + k + 1])
                    ins.then_inc(mod_hi, 1)

            def keep_v(m):
                act.wait_ge(v_turned, m + 1)
                nc.scalar.copy(proj[:, AV + m if m < HEADS else RV + m - HEADS, :],
                               ps[:, 7, 0:T]).then_inc(v_kept, 1)

            def exp(h):
                act.wait_ge(max_ready, h + 1)
                e = att_buf(s0, h)
                nc.scalar.activation(e[:, 0:P], e[:, 0:P], ACT.Exp, bias=nmx[:, h % 2, 0:1])
                nc.scalar.activation(e[:, P:3 * P], e[:, P:3 * P], ACT.Exp, bias=nmx[:, h % 2, 1:2]).then_inc(exp_ready, 1)

            def keep_p(h):
                act.wait_ge(pt_done, h + 1)
                if h >= 2:
                    act.wait_ge(ao_done, h - 1)
                nc.scalar.copy(att_buf(s1, h), ps[:, 5, 0:3 * P]).then_inc(pt_kept, 1)

            def att_hi(h):
                act.wait_ge(ao_done, h + 1)
                nc.scalar.copy(y_split(h)[0], ps[:, 6, 0:T]).then_inc(y_hi, 1)

            def keep_o(h):
                act.wait_ge(ro_done, h + 1)
                nc.scalar.copy(proj[:, RV + h, :], ps[:, 5, 0:T]).then_inc(ro_kept, 1)

            def std(half):
                act.wait_ge(var_ready, half + 1)
                c = slice(HEADS * half, HEADS * half + HEADS)
                nc.scalar.activation(var[:, 2, c], var[:, 1, c], ACT.Sqrt).then_inc(std_ready, 1)

            def silu(half):
                act.wait_ge(in_kept, SETS + IN0[HEADS_AT + 1] - 1 + half)
                g = proj[:, RG + 4 * half:RG + 4 * half + 4, :]
                nc.scalar.activation(g, g, ACT.Silu).then_inc(g_silu, 1)

            def ret_hi(h):
                act.wait_ge(y_ret, h + 1)
                nc.scalar.copy(y_split(HEADS + h)[0], proj[:, RG + h, :]).then_inc(y_hi, 1)

            act.wait_ge(const_in, 64)
            nc.scalar.activation(cc[:, 1, :], cc[:, 0, :], ACT.Silu).then_inc(c_ready, 1)
            act.wait_ge(x_loaded, 16)
            for q in range(QUARTERS):
                if q > 0:
                    act.wait_ge(part_ready, q)
                square(0, NT * q, q)
            take_root(0)
            modulate(0, range(2))
            for c in range(4):
                w_hi(c, c // RING, c % RING)
            for q in range(1, QUARTERS):
                for c in range(4 * q, 4 * q + 4):
                    w_hi(c, c // RING, c % RING)
                modulate(0, range(2 * q, 2 * q + 2))

            def take_gate(done):
                act.wait_ge(w_free, done)
                nc.scalar.activation(s1[:, :, :], group_out(0), ACT.Silu).then_inc(silu_ready, 1)

            def hid_hi_part(i, p, it):
                act.wait_ge(hid_f32, it + (HID0[i] + 2))
                nc.scalar.copy(hid[:, bass.ds(it * NT + p.tile0, NT), 0:T], s3[:, :, :]).then_inc(hid_hi, 1)

            for c in range(PHASES[0].chunks, PHASES[0].chunks + RING):
                if c == PHASES[0].chunks + 2:
                    take_gate(RING + PHASES[0].chunks - 2)
                w_hi(c, c // RING, c % RING)
            hid_hi_part(0, PHASES[0], 0)

            def body(i, p, it, peeled, follow):
                def res_squares(g):
                    act.wait_ge(res_step, it * 2 + (SETS + RES0[i] + g + 1))
                    square(p.squares, it * 2 * NT + g * NT, it * 2 + (QUARTERS * p.squares + g))

                for j in ahead_range(i, peeled):
                    if p.kind == UP and j == p.group_chunks:
                        take_gate(group_end(i, it, 0))
                    if p.squares is not None and j == p.group_chunks + 1:
                        res_squares(0)
                    number, uses = ahead(i, it, j)
                    w_hi(number, uses, j % RING)
                    if follow:
                        follow(it * p.chunks + j)
                if p.kind == UP:
                    hid_hi_part(i, p, it)
                if p.squares is not None:
                    res_squares(1)

            def after(i, p):
                if p.squares is not None:
                    take_root(p.squares)
                    if p.squares < 3:
                        modulate(p.squares, range(DT // 2))

            run_phases(act, body, {"turn_v": keep_v, "exp": exp, "turn_p": keep_p, "attend": att_hi,
                                   "ret_out": keep_o, "std": std, "silu": silu, "split_ret": ret_hi}, after)

        @block.vector
        def _(dve):
            steps = [0]

            def then(ins):
                steps[0] += 1
                ins.then_inc(dve_step, 1)
                dve.wait_ge(dve_step, steps[0])

            def w_lo(number, slot):
                dve.wait_ge(hi_ready, number + 1)
                nc.vector.tensor_tensor(wlo[:, slot, :], raw[:, slot, :], whi[:, slot, :].bitcast(F32),
                                        ALU.subtract).then_inc(lo_ready, 1)

            def ada_mac(group, k, slot):
                chunk = k // KC
                src = araw[:, chunk % RING, (k % KC) * GW:(k % KC) * GW + GW]
                dst = acc[:, bass.ds(slot, 1), :].rearrange("p a n -> p (a n)")
                if k % KC == 0:
                    dve.wait_ge(ada_in[chunk % RING],
                                group * (16 * ADA_CHUNKS // RING)
                                + (chunk // RING + 1 - ADA_FIRST * ADA_CHUNKS // RING) * 16)
                if k == 0:
                    nc.vector.tensor_scalar(dst, src, cc[:, 1, 0:1], None, ALU.mult).then_inc(ada_step, 1)
                else:
                    dve.wait_ge(ada_step, group * ADA_STEPS + (2 * RING + k))
                    nc.vector.scalar_tensor_tensor(out=dst, in0=src, scalar=cc[:, 1, k:k + 1], in1=dst,
                                                   op0=ALU.mult, op1=ALU.add).then_inc(ada_step, 1)

            def ada_half(n, chunk):
                number = ADA_CHUNKS * n + chunk
                dve.wait_ge(early_in[number % EARLY_RING], 16 * (number // EARLY_RING + 1))
                for k in range(KC * chunk, KC * chunk + KC):
                    src, dst = ada_early[:, number % EARLY_RING, (k % KC) * GW:(k % KC) * GW + GW], acc[:, n % 2, :]
                    if k == 0:
                        ins = nc.vector.tensor_scalar(dst, src, cc[:, 1, 0:1], None, ALU.mult)
                    else:
                        dve.wait_ge(ada_step, 2 * RING + n * ADA_STEPS + KC * chunk + 2 * (k % KC))
                        ins = nc.vector.scalar_tensor_tensor(out=dst, in0=src, scalar=cc[:, 1, k:k + 1], in1=dst,
                                                             op0=ALU.mult, op1=ALU.add)
                    ins.then_inc(ada_step, 2)

            def ada_merge(n):
                dve.wait_ge(ada_used, ADA_CHUNKS // 2 * (n + 1))
                dve.wait_ge(ada_step, 2 * RING + (n + 1) * ADA_STEPS)
                nc.vector.tensor_tensor(acc[0:1, n % 2, :], ps[0:1, row_bank(n), :], acc[0:1, n % 2, :],
                                        ALU.add).then_inc(ada_merged, 1)

            def ada_keep(rnd, dst, n):
                dve.wait_ge(ada_turned, rnd + 1)
                nc.vector.tensor_reduce(asum[:, 0:n * NT], ps[:, 6:6 + n, :].rearrange("p b (n q) -> p (b n) q", q=P),
                                        AX.X, ALU.add).then_inc(asum_ready, 1)
                dve.wait_ge(asum_ready, rnd + 1)
                total = asum[:, 0:n * NT]
                if len(dst.shape) == 3:
                    total = total.rearrange("p (b n) -> p b n", b=n)
                nc.vector.tensor_tensor(dst, total, dst, ALU.add).then_inc(ada_out, 1)

            def set_gate(layer, factor):
                c = slice((3 * layer + 2) * DT, (3 * layer + 3) * DT)
                then(nc.vector.tensor_scalar(gate[:, :], ada[:, c], factor, None, ALU.mult))

            def sum_squares(dst_q, step):
                dve.wait_ge(sq_ready, step + 1)
                nc.vector.tensor_reduce(s0[:, bass.ds(dst_q, 1), :].rearrange("p a t -> p (a t)"),
                                        s2[:, :, :].rearrange("p a t -> p t a"), AX.X, ALU.add).then_inc(part_ready, 1)

            def inverse_root(n):
                dve.wait_ge(root_ready, n + 1)
                then(nc.vector.reciprocal(rms[:, :], root[:, :]))

            def mod_scale(n, tiles, rounds):
                dve.wait_ge(ada_out, rounds)
                a = (3 * n + 1) * DT
                nc.vector.scalar_tensor_tensor(out=scl[:, tiles], in0=ada[:, a + tiles.start:a + tiles.stop], scalar=1.0,
                                               in1=gain[:, n, tiles], op0=ALU.add, op1=ALU.mult).then_inc(scl_ready, 1)

            def modulate(n, pairs):
                def lo(j):
                    dve.wait_ge(mod_hi, 8 * n + j + 1)
                    for t in range(2):
                        k = 2 * j + t
                        ins = nc.vector.scalar_tensor_tensor(
                            out=xsp[:, k, T:2 * T], in0=scaled(j)[:, t, :],
                            scalar=ada[:, 3 * n * DT + k:3 * n * DT + k + 1],
                            in1=xsp[:, k, 0:T].bitcast(F32), op0=ALU.add, op1=ALU.subtract)
                    ins.then_inc(mod_ready, 1)

                dve.wait_ge(scl_ready, pairs[0] // 2 + 1 if n == 0 else QUARTERS + n)
                for j in pairs:
                    if j >= 4:
                        dve.wait_ge(mod_ready, 8 * n + j - 3)
                    for t in range(2):
                        k = 2 * j + t
                        ins = nc.vector.scalar_tensor_tensor(out=scaled(j)[:, t, :], in0=xs[:, k, :],
                                                             scalar=scl[:, k:k + 1], in1=rms[:, :],
                                                             op0=ALU.mult, op1=ALU.mult)
                    ins.then_inc(xn_ready, 1)
                    if j > pairs[0]:
                        lo(j - 1)
                lo(pairs[-1])

            def take_group(i, p, it, g):
                if p.kind == UP and g == 0:
                    return
                dve.wait_ge(w_free, group_end(i, it, g))
                r = group_out(g)
                if p.kind == UP:
                    dve.wait_ge(silu_ready, it + (HID0[i] + 2))
                    nc.vector.tensor_tensor(s3[:, :, :], s1[:, :, :], r, ALU.mult).then_inc(hid_f32, 1)
                elif p.kind == IN:
                    nc.vector.tensor_copy(proj[:, bass.ds(it * 2 * NT + (p.tile0 + g * NT), NT), :], r).then_inc(in_kept, 1)
                else:
                    for n in range(NT):
                        tile = it * 2 * NT + (g * NT + n)
                        x = xs[:, bass.ds(tile, 1), :].rearrange("p a t -> p (a t)")
                        ins = nc.vector.scalar_tensor_tensor(out=x, in0=r[:, n, :], scalar=gate[:, bass.ds(tile, 1)],
                                                             in1=x, op0=ALU.mult, op1=ALU.add)
                    ins.then_inc(res_step, 1)

            def hid_lo(i, p, it):
                dve.wait_ge(hid_hi, it + (HID0[i] + 1))
                tiles = bass.ds(it * NT + p.tile0, NT)
                nc.vector.tensor_tensor(hid[:, tiles, T:2 * T], s3[:, :, :], hid[:, tiles, 0:T].bitcast(F32),
                                        ALU.subtract).then_inc(hid_ready, 1)

            def mask_scores(h):
                dve.wait_ge(sc_done, h + 1)
                if h >= 2:
                    dve.wait_ge(pt_done, h - 1)
                e = att_buf(s0, h)
                nc.vector.scalar_tensor_tensor(out=e, in0=ps[:, 4, 0:3 * P], scalar=ATT_SCALE, in1=mask,
                                               op0=ALU.mult, op1=ALU.add).then_inc(sc_masked, 1)
                dve.wait_ge(sc_masked, h + 1)
                nc.vector.tensor_reduce(mx[:, h % 2, 0:1], e[:, 0:P], AX.X, ALU.max)
                then(nc.vector.tensor_reduce(mx[:, h % 2, 1:2], e[:, P:3 * P], AX.X, ALU.max))
                nc.vector.tensor_scalar(nmx[:, h % 2, :], mx[:, h % 2, :], -1.0, None, ALU.mult).then_inc(max_ready, 1)

            def probs(h):
                dve.wait_ge(exp_ready, h + 1)
                e = att_buf(s0, h)
                cuts = enumerate((slice(0, P), slice(P, 3 * P)))
                for b, cut in cuts:
                    ins = nc.vector.tensor_tensor_reduce(e[:, cut], e[:, cut], count[:, cut], 1.0, 0.0, ALU.mult,
                                                         ALU.add, den[:, h % 2, b:b + 1])
                then(ins)
                then(nc.vector.reciprocal(rden[:, h % 2, :], den[:, h % 2, :]))
                for b, cut in enumerate((slice(0, P), slice(P, 3 * P))):
                    ins = nc.vector.tensor_scalar(e[:, cut], e[:, cut], rden[:, h % 2, b:b + 1], None, ALU.mult)
                ins.then_inc(p_ready, 1)

            def rotated(j):
                dve.wait_ge(rot_done, j + 1)
                if j >= 1:
                    dve.wait_ge(rot_kept, j)
                x = proj[:, RQ + j, :]
                nc.vector.tensor_tensor(s3[:, 0, :], x, cos, ALU.mult)
                then(nc.vector.tensor_tensor(s3[:, 1, :], ps[:, 6, 0:T], sin, ALU.mult))
                nc.vector.tensor_tensor(x, s3[:, 0, :], s3[:, 1, :], ALU.add).then_inc(rot_kept, 1)

            def decayed(h):
                dve.wait_ge(ra_done, h + 1)
                if h >= 2:
                    dve.wait_ge(ro_done, h - 1)
                a, dec = att_buf(s2, h), tb["decay"][:, h * T:h * T + T]
                nc.vector.tensor_tensor(a[:, 0:T], ps[:, 4, 0:T], dec, ALU.mult)
                nc.vector.tensor_tensor(a[:, T:T + P], ps[:, 4, T:T + P], dec[:, 0:P], ALU.mult).then_inc(ra_kept, 1)

            def head_stats(h):
                dve.wait_ge(ro_kept, h + 1)
                nc.vector.bn_stats(stats[:, 0, :], proj[:, RV + h, 0:P])
                then(nc.vector.bn_stats(stats[:, 1, :], proj[:, RV + h, P:T]))
                nc.vector.bn_aggr(mv[:, 2 * h, :], stats[:, 0, :])
                then(nc.vector.bn_aggr(mv[:, 2 * h + 1, :], stats[:, 1, :]))

            def inverse_var(half):
                c = slice(HEADS * half, HEADS * half + HEADS)
                then(nc.vector.tensor_scalar(var[:, 0, c], mv[:, c, 1], EPS, None, ALU.add))
                nc.vector.reciprocal(var[:, 1, c], var[:, 0, c]).then_inc(var_ready, 1)

            def norm_o(h):
                dve.wait_ge(std_ready, h // 4 + 1)
                for t in range(2):
                    o, m = proj[:, RV + h, t * P:t * P + P], 2 * h + t
                    ins = nc.vector.tensor_scalar(o, o, mv[:, m, 0:1], var[:, 2, m:m + 1], ALU.subtract, ALU.mult)
                ins.then_inc(ro_norm, 1)

            def gated(h):
                dve.wait_ge(rt_done, h // 2 * 2 + 2)
                dve.wait_ge(g_silu, h // 4 + 1)
                g = proj[:, RG + h, :]
                nc.vector.tensor_tensor(g, turned_o(h), g, ALU.mult).then_inc(y_ret, 1)

            def heads_ada(n):
                group = ADA0[HEADS_AT] + n
                ada_keep(ROUND0[HEADS_AT] + n, ada[:, group * NT:(group + 1) * NT], 1)

            def att_lo(h):
                dve.wait_ge(y_hi, h + 1)
                hi, lo = y_split(h)
                nc.vector.tensor_tensor(lo, ps[:, 6, 0:T], hi.bitcast(F32), ALU.subtract).then_inc(y_ready, 1)

            def ret_lo(h):
                dve.wait_ge(y_hi, HEADS + h + 1)
                hi, lo = y_split(HEADS + h)
                nc.vector.tensor_tensor(lo, proj[:, RG + h, :], hi.bitcast(F32), ALU.subtract).then_inc(y_ready, 1)

            nc.vector.memset(credit[:, 0:1], 0.0).then_inc(lo_ready, RING)
            nc.vector.memset(credit[:, 1:2], 0.0).then_inc(w_free, RING)
            nc.vector.memset(credit[:, 2:3], 0.0).then_inc(ada_step, 2 * RING)
            nc.vector.memset(credit[:, 3:4], 0.0).then_inc(in_kept, SETS)
            nc.vector.memset(credit[:, 4:5], 0.0).then_inc(res_step, SETS)
            nc.vector.memset(credit[:, 5:6], 0.0).then_inc(silu_ready, 1)
            nc.vector.memset(credit[:, 6:7], 0.0).then_inc(hid_f32, 1)
            dve.wait_ge(c_ready, 1)
            for q in range(QUARTERS):
                for n in range(2 * q, 2 * q + 2):
                    for k in range(0, ADA_CHUNKS, 2):
                        ada_half(n, k)
                        if n == 1:
                            sum_squares(k // 2, k // 2)
                        if n > 1 and n % 2 == 1 and k > 0:
                            for c in range(4 * q if k == 2 else 4 * q + k // 2, 4 * q + k // 2 + 1):
                                w_lo(c, c % RING)
                        if n % 2 == 1 and k == 4:
                            ada_merge(n - 1)
                ada_merge(2 * q + 1)
                ada_keep(q, ada[:, 0:2 * DT].rearrange("p (v m) -> p v m", v=2)[:, :, NT * q:NT * q + NT], 2)
                if q == 0:
                    inverse_root(0)
                mod_scale(0, slice(NT * q, NT * q + NT), q + 1)
                modulate(0, range(2 * q, 2 * q + 2))
                if q == 0:
                    for c in range(4):
                        w_lo(c, c % RING)
            for c in range(PHASES[0].chunks, PHASES[0].chunks + RING):
                w_lo(c, c % RING)
            take_group(0, PHASES[0], 0, 1)
            hid_lo(0, PHASES[0], 0)

            def body(i, p, it, peeled, follow):
                def res_squares(g):
                    sum_squares(it * 2 + g, it * 2 + (QUARTERS * p.squares + g))

                for j in ahead_range(i, peeled):
                    if j == p.group_chunks:
                        take_group(i, p, it, 0)
                    if j == p.chunks - 1:
                        take_group(i, p, it, 1)
                    if follow:
                        follow(it * p.chunks + j)
                    w_lo(ahead(i, it, j)[0], j % RING)
                    if p.squares is not None and j == p.group_chunks + 2:
                        res_squares(0)
                    for s in ada_part(p, it, j, ADA_STEPS):
                        if p.heads:
                            n = s // ADA_STEPS
                            ada_mac(ADA0[i] + n, s % ADA_STEPS, n % ACC)
                        else:
                            ada_mac(it * p.ada + (ADA0[i] + s // ADA_STEPS), s % ADA_STEPS, s // ADA_STEPS)
                if peeled:
                    take_group(i, p, it, 1)
                if p.kind == UP:
                    hid_lo(i, p, it)
                if p.squares is not None:
                    res_squares(1)
                if p.ada and not p.heads:
                    ada_keep(it + ROUND0[i], ada[:, bass.ds(it * (p.ada * NT) + ADA0[i] * NT, p.ada * NT)], p.ada)

            def after(i, p):
                if i in GATE_AFTER:
                    dve.wait_ge(ada_out, ROUND0[i + 1])
                    set_gate(*GATE_AFTER[i])
                if p.squares is not None:
                    if p.squares < 3:
                        mod_scale(p.squares, slice(0, DT), ROUND0[i + 1])
                    inverse_root(p.squares)
                    if p.squares < 3:
                        modulate(p.squares, range(DT // 2))

            run_phases(dve, body, {"mask": mask_scores, "probs": probs, "rotate": rotated, "ret_scores": decayed,
                                   "stats": head_stats, "std": inverse_var, "norm_o": norm_o, "gate": gated,
                                   "split_att": att_lo, "split_ret": ret_lo, "ada": heads_ada}, after)
            for k in range(DT):
                ins = nc.vector.scalar_tensor_tensor(out=xs[:, k, :], in0=xs[:, k, :], scalar=gain[:, 3, k:k + 1],
                                                     in1=rms[:, :], op0=ALU.mult, op1=ALU.mult)
                if k % 4 == 3:
                    ins.then_inc(out_ready, 1)

        @block.tensor
        def _(pe):
            def halves(x):
                return lambda k: (x[:, k, 0:T], x[:, k, T:2 * T])

            def group_chunk(slot, x, k0, bank, last_k):
                for k in range(k0, k0 + KC):
                    x_hi, x_lo = x(k)
                    for n in range(NT):
                        at = (k - k0) * GW + n * P
                        o = ps[:, bank + n // 2, (n % 2) * T:(n % 2) * T + T]
                        hi, lo = whi[:, slot, at:at + P], wlo[:, slot, at:at + P]
                        nc.tensor.matmul(o, hi, x_hi, start=(k == 0 and n % 2 == 0), stop=False, skip_group_check=True)
                        nc.tensor.matmul(o, hi, x_lo, start=False, stop=False, skip_group_check=True)
                        ins = nc.tensor.matmul(o, lo, x_hi, start=False, stop=(k == last_k), skip_group_check=True)
                return ins

            def ada_turn(rnd, total, n, first=0):
                pe.wait_ge(ada_step, total * ADA_STEPS + 2 * RING)
                if rnd is not None:
                    pe.wait_ge(ada_out, rnd)
                for m in range(n):
                    for t in range(NT):
                        ins = nc.tensor.transpose(ps[:, 6 + m, t * P:t * P + P], acc[:, first + m, t * P:t * P + P], ident)
                ins.then_inc(ada_turned, 1)

            def mean(n):
                for q in range(QUARTERS):
                    pe.wait_ge(part_ready, QUARTERS * n + q + 1)
                    ins = nc.tensor.matmul(ps[:, MISC, 0:T], ones_mean, s0[:, q, :], start=(q == 0),
                                           stop=(q == QUARTERS - 1))
                ins.then_inc(mean_ready, 1)

            def turn_v(m):
                if m >= HEADS:
                    pe.wait_ge(in_kept, SETS + IN0[HEADS_AT] + 3 + (m - HEADS) // 4)
                if m >= 1:
                    pe.wait_ge(v_kept, m)
                v = proj[:, AV + m if m < HEADS else RV + m - HEADS, :]
                for t in range(2):
                    ins = nc.tensor.transpose(ps[:, 7, t * P:t * P + P], v[:, t * P:t * P + P], ident)
                ins.then_inc(v_turned, 1)

            def scores(h):
                if h == 0:
                    pe.wait_ge(table_in, 16)
                pe.wait_ge(in_kept, SETS + IN0[HEADS_AT])
                if h >= 1:
                    pe.wait_ge(sc_masked, h)
                q, k = proj[:, AQ + h, :], proj[:, AK + h, :]
                nc.tensor.matmul(ps[:, 4, 0:P], q[:, 0:P], k[:, 0:P], start=True, stop=True)
                nc.tensor.matmul(ps[:, 4, P:3 * P], q[:, P:T], k, start=True, stop=True).then_inc(sc_done, 1)

            def turn_p(h):
                pe.wait_ge(p_ready, h + 1)
                if h >= 1:
                    pe.wait_ge(pt_kept, h)
                e = att_buf(s0, h)
                for b in range(3):
                    ins = nc.tensor.transpose(ps[:, 5, b * P:b * P + P], e[:, b * P:b * P + P], ident)
                ins.then_inc(pt_done, 1)

            def attend(h):
                pe.wait_ge(pt_kept, h + 1)
                pe.wait_ge(v_kept, h + 1)
                if h >= 1:
                    pe.wait_ge(y_ready, h)
                rotated = sum(chunk < 3 * h + 4 for chunk in ROTATE_AT)
                if rotated:
                    pe.wait_ge(rot_kept, rotated)
                pt, v = att_buf(s1, h), proj[:, AV + h, :]
                nc.tensor.matmul(ps[:, 6, 0:T], v[:, 0:P], pt[:, 0:T], start=True, stop=False, skip_group_check=True)
                nc.tensor.matmul(ps[:, 6, P:T], v[:, P:T], pt[:, T:T + P], start=False, stop=True,
                                 skip_group_check=True).then_inc(ao_done, 1)

            def rotate_tile(j):
                pe.wait_ge(in_kept, SETS + IN0[HEADS_AT] + j // 4 + 1)
                pe.wait_ge(y_ready, sum(3 * h + 4 <= ROTATE_AT[j] for h in range(HEADS)))
                if j >= 1:
                    pe.wait_ge(rot_kept, j)
                nc.tensor.matmul(ps[:, 6, 0:T], rotate, proj[:, RQ + j, :], start=True, stop=True).then_inc(rot_done, 1)

            def ret_scores(h):
                if h == 0:
                    pe.wait_ge(rot_kept, HEADS)
                    pe.wait_ge(sc_masked, HEADS)
                else:
                    pe.wait_ge(ra_kept, h)
                rows = slice(DK * (h % 2), DK * (h % 2) + DK)
                q, k = proj[rows, RQ + h // 2, :], proj[rows, RK + h // 2, :]
                nc.tensor.matmul(ps[:, 4, 0:T], k[:, 0:P], q, start=True, stop=True)
                nc.tensor.matmul(ps[:, 4, T:T + P], k[:, P:T], q[:, P:T], start=True, stop=True).then_inc(ra_done, 1)

            def ret_out(h):
                pe.wait_ge(ra_kept, h + 1)
                pe.wait_ge(v_kept, HEADS + h + 1)
                if h == 0:
                    pe.wait_ge(pt_kept, HEADS)
                else:
                    pe.wait_ge(ro_kept, h)
                a, v = att_buf(s2, h), proj[:, RV + h, :]
                nc.tensor.matmul(ps[:, 5, 0:P], a[:, 0:P], v[:, 0:P], start=True, stop=True)
                nc.tensor.matmul(ps[:, 5, P:T], a[:, P:T], v[:, 0:P], start=True, stop=False)
                nc.tensor.matmul(ps[:, 5, P:T], a[:, T:T + P], v[:, P:T], start=False, stop=True).then_inc(ro_done, 1)

            def turn_o(h):
                pe.wait_ge(ro_norm, h + 1)
                if h < 2:
                    pe.wait_ge(v_kept, 2 * HEADS)
                elif h < 4:
                    pe.wait_ge(y_ret, 2)
                else:
                    pe.wait_ge(ra_kept if h < 6 else ro_kept, HEADS)
                for t in range(2):
                    ins = nc.tensor.transpose(turned_o(h)[:, t * P:t * P + P], proj[:, RV + h, t * P:t * P + P], ident)
                ins.then_inc(rt_done, 1)

            def heads_ada(n):
                pe.wait_ge(y_ready, HEADS)
                pe.wait_ge(rot_kept, HEADS)
                ada_turn(ROUND0[HEADS_AT] + n, ADA0[HEADS_AT] + n + 1, 1, n % ACC)

            def ada_half(n, chunk):
                if chunk == 1 and n >= 2:
                    pe.wait_ge(ada_merged, n - 1)
                    pe.wait_ge(ada_out, n // 2)
                number = ADA_CHUNKS * n + chunk
                pe.wait_ge(early_in[number % EARLY_RING], 16 * (number // EARLY_RING + 1))
                for k in range(KC):
                    ins = nc.tensor.matmul(ps[0:1, row_bank(n), :], cc[:, 1, KC * chunk + k:KC * chunk + k + 1],
                                           ada_early[:, number % EARLY_RING, k * GW:k * GW + GW],
                                           start=(chunk == 1 and k == 0),
                                           stop=(chunk == ADA_CHUNKS - 1 and k == KC - 1))
                ins.then_inc(ada_used, 1)

            def first_chunk(c):
                g, k0 = c % 4 // 2, NT * (c // 4) + KC * (c % 2)
                pe.wait_ge(lo_ready, RING + c + 1)
                pe.wait_ge(mod_ready, k0 // 2 + 1)
                group_chunk(c % RING, halves(xsp), k0, 2 * g, DT - 1).then_inc(w_free, 1)

            pe.wait_ge(const_in, 64)
            pe.wait_ge(c_ready, 1)
            for q in range(QUARTERS):
                for n in range(2 * q, 2 * q + 2):
                    for k in range(1, ADA_CHUNKS, 2):
                        ada_half(n, k)
                        if q > 0 and n == 2 * q:
                            for c in {3: (0, 1, 2), 5: (3,)}.get(k, ()):
                                first_chunk(4 * (q - 1) + c)
                if q == 0:
                    mean(0)
                pe.wait_ge(ada_merged, 2 * q + 2)
                ada_turn(q if q else None, 2 * q + 2, 2)
            for c in range(4 * QUARTERS - 4, 4 * QUARTERS):
                first_chunk(c)

            def set_out(i, bodies, g):
                if PHASES[i].kind == UP:
                    pe.wait_ge(hid_f32 if g else silu_ready, bodies + (HID0[i] + 1))
                elif PHASES[i].kind == IN:
                    pe.wait_ge(in_kept, bodies * 2 + (SETS - 1 + g + IN0[i]))
                else:
                    pe.wait_ge(res_step, bodies * 2 + (SETS - 1 + g + RES0[i]))

            def body(i, p, it, peeled, follow):
                x = y_split if p.kind == OUT else halves(hid if p.kind == DOWN else xsp)
                for g in range(2):
                    if i > 0:
                        set_out(i - 1, PHASES[i - 1].bodies, g)
                    set_out(i, it, g)
                    for j in range(p.group_chunks):
                        c = g * p.group_chunks + j
                        pe.wait_ge(lo_ready, it * p.chunks + (RING + CHUNK0[i] + c + 1))
                        if p.norm is not None and g == 0:
                            pe.wait_ge(mod_ready, 8 * p.norm + j + 1)
                        if p.kind == OUT and g == 0:
                            pe.wait_ge(y_ready, KC * (j + 1))
                        if p.kind == DOWN and g == 0 and j in (0, p.group_chunks - 2):
                            pe.wait_ge(hid_ready, HID0[i] - (j == 0))
                        group_chunk(c % RING, x, KC * j, 2 * g, KC * p.group_chunks - 1).then_inc(w_free, 1)
                        if follow:
                            follow(it * p.chunks + c)
                if p.ada and not p.heads:
                    ada_turn(it + ROUND0[i], it * p.ada + (ADA0[i] + p.ada), p.ada)

            def after(i, p):
                if p.squares is not None:
                    mean(p.squares)

            run_phases(pe, body, {"turn_v": turn_v, "scores": scores, "turn_p": turn_p, "attend": attend,
                                  "rotate": rotate_tile, "ret_scores": ret_scores, "ret_out": ret_out,
                                  "turn_o": turn_o, "ada": heads_ada}, after, peel=False)


def chunks(w):
    k, n = w.shape
    return w.reshape(k // (KC * P), KC, P, n // GW, GW).transpose(3, 0, 2, 1, 4).reshape(n // GW, k // (KC * P), P, CH)


def columns(v):
    return np.ascontiguousarray(v.reshape(-1, P).T)


def weights_in_order(w1_gate, w1_up, w1_down, w_in, w_out, w2_gate, w2_up, w2_down):
    total = sum(p.chunks * p.bodies for p in PHASES)
    flat = np.empty((total, P, CH), np.float32)
    at = 0

    def put(part):
        nonlocal at
        part = part.reshape(-1, P, CH)
        flat[at:at + len(part)] = part
        at += len(part)

    def swiglu(gate, up, down):
        gate, up, down = chunks(gate), chunks(up), chunks(down)
        cut = FA * NT // KC
        for first, last in ((0, FA), (FA, FA + FB)):
            for g in range(first, last):
                both = np.stack([gate[g], up[g]])
                if at == 0:
                    both = both.reshape(2, QUARTERS, 2, P, CH).transpose(1, 0, 2, 3, 4)
                put(both)
            put(down[:, :cut] if first == 0 else down[:, cut:])

    swiglu(w1_gate, w1_up, w1_down)
    put(chunks(w_in))
    put(chunks(w_out))
    swiglu(w2_gate, w2_up, w2_down)
    return flat


def kernel(x, c, w_ada, b_ada, g_ffn1, w1_gate, w1_up, w1_down, g_mix, w_in, w_out,
           g_ffn2, w2_gate, w2_up, w2_down, g_final):
    import concourse.bacc as _bacc
    from concourse.bass_utils import run_bass_kernel_spmd as _run

    nc = _bacc.Bacc("TRN2", target_bir_lowering=False, num_devices=1)
    arrays = {
        "x_t": np.ascontiguousarray(x[0].T.reshape(DT, P, T).transpose(1, 0, 2)),
        "c_t": columns(c[0]),
        "w_ada_chunks": chunks(w_ada[0])[ADA_ORDER].reshape(-1, P, CH),
        "b_ada_t": columns(b_ada[0]),
        "gains_t": np.stack([columns(g_ffn1[0]), columns(g_mix[0]), columns(g_ffn2[0]), columns(g_final)], 1),
        "w_chunks": weights_in_order(w1_gate[0], w1_up[0], w1_down[0], w_in[0], w_out[0], w2_gate[0], w2_up[0],
                                     w2_down[0]),
        "tables": tables(),
    }
    args = [nc.dram_tensor(name, a.shape, F32, kind="ExternalInput").ap() for name, a in arrays.items()]
    out = nc.dram_tensor("out_t", (P, DT, T), F32, kind="ExternalOutput").ap()
    build(nc, *args, out)
    r = _run(nc, [arrays], core_ids=[0])
    got = r.results[0]["out_t"]
    return np.ascontiguousarray(got.transpose(1, 0, 2).reshape(D, T).T)[None]
```
